# Optimizing a Trainium2 kernel written in Bass

```python
import math
import jax, jax.numpy as jnp
from jax import lax
import numpy as np

D_MODEL = 1024
BATCH = 1
SEQ = 256
DEPTH = 1

N_MEM = 256
N_HEADS_A = 8
HEAD_DIM_A = 64
WIDTH_A = N_HEADS_A * HEAD_DIM_A
DILATED_PATTERNS = ((128, 1), (512, 4), (2048, 16))
N_HEADS_B = 8
QK_NOPE_DIM = 64
QK_ROPE_DIM = 32
V_DIM_B = 64
WIDTH_B = N_HEADS_B * V_DIM_B
Q_LORA_RANK = 256
KV_LORA_RANK = 128
ROPE_THETA = 10000.0
MIX_WIDTH = WIDTH_A + WIDTH_B
IN_PROJ_WIDTH = 3 * WIDTH_A + Q_LORA_RANK + KV_LORA_RANK + QK_ROPE_DIM
NUM_BUCKETS = 32
MAX_DISTANCE = 1024
N_HEADS_MEM = 4
HEAD_DIM_MEM = D_MODEL // N_HEADS_MEM
N_EXPERTS = 32
TOP_K = 4
D_EXPERT = D_MODEL
SWIGLU_LIMIT = 7.0
SWIGLU_ALPHA = 1.702
EXPERT_BLOCK = 256
Q_BLOCK = 128
EPS = 1e-6
NEG_INF = -1e30

kernel_name = "hybrid_dilated_mla_moe_encoder"

def rmsnorm(x, g):
    xf = x.astype(jnp.float32)
    y = xf * lax.rsqrt(jnp.mean(xf * xf, axis=-1, keepdims=True) + EPS)
    return (y * g.astype(jnp.float32)).astype(x.dtype)

def rope_cos_sin(positions):
    inv_freq = ROPE_THETA ** (-jnp.arange(0, QK_ROPE_DIM, 2, dtype=jnp.float32) / QK_ROPE_DIM)
    ang = positions.astype(jnp.float32)[..., None] * inv_freq
    return jnp.cos(ang), jnp.sin(ang)

def apply_rope(x, cos, sin):
    x1, x2 = jnp.split(x.astype(jnp.float32), 2, axis=-1)
    return jnp.concatenate([x1 * cos - x2 * sin, x1 * sin + x2 * cos], axis=-1).astype(x.dtype)

def rel_bucket(rel):
    nb = NUM_BUCKETS // 2
    max_exact = nb // 2
    ret = (rel > 0).astype(jnp.int32) * nb
    n = jnp.abs(rel)
    nf = jnp.maximum(n, max_exact).astype(jnp.float32)
    large = max_exact + (jnp.log(nf / max_exact) / math.log(MAX_DISTANCE / max_exact)
                         * (nb - max_exact)).astype(jnp.int32)
    large = jnp.minimum(large, nb - 1)
    return ret + jnp.where(n < max_exact, n, large)

def dilated_attention(q, k, v, positions, rel_bias):
    b, s = q.shape[:2]
    n_blocks = s // Q_BLOCK
    scale = HEAD_DIM_A ** -0.5

    def block(i):
        q0 = i * Q_BLOCK
        qb = lax.dynamic_slice_in_dim(q, q0, Q_BLOCK, axis=1)
        qpos = lax.dynamic_slice_in_dim(positions, q0, Q_BLOCK, axis=1)
        qidx = q0 + jnp.arange(Q_BLOCK)
        outs, lses = [], []
        for window, dil in DILATED_PATTERNS:
            half = window // (2 * dil)
            offs = jnp.arange(-half, half + 1) * dil
            kidx = qidx[:, None] + offs[None, :]
            valid = (kidx >= 0) & (kidx < s)
            kidx = jnp.clip(kidx, 0, s - 1)
            kg = k[:, kidx]
            vg = v[:, kidx]
            rel = positions[:, kidx] - qpos[:, :, None]
            bias = rel_bias[rel_bucket(rel)]
            sc = (jnp.einsum('bqhd,bqkhd->bqkh', qb, kg).astype(jnp.float32) * scale
                  + bias.astype(jnp.float32))
            sc = jnp.where(valid[None, :, :, None], sc, NEG_INF)
            lse = jax.nn.logsumexp(sc, axis=2)
            p = jnp.exp(sc - lse[:, :, None, :])
            outs.append(jnp.einsum('bqkh,bqkhd->bqhd', p, vg.astype(jnp.float32)))
            lses.append(lse)
        wts = jax.nn.softmax(jnp.stack(lses, axis=0), axis=0)
        o = jnp.sum(wts[..., None] * jnp.stack(outs, axis=0), axis=0)
        return o.astype(q.dtype)

    o = lax.map(block, jnp.arange(n_blocks))
    return o.transpose(1, 0, 2, 3, 4).reshape(b, s, WIDTH_A)

def mla_attention(q_nope, q_pe, k_nope, k_pe, v):
    b, s = q_nope.shape[:2]
    nb = s // Q_BLOCK
    scale = (QK_NOPE_DIM + QK_ROPE_DIM) ** -0.5

    def to_blocks(t):
        return t.reshape(b, nb, Q_BLOCK, *t.shape[2:]).swapaxes(0, 1)

    def block(args):
        qn, qp = args
        sc = (jnp.einsum('bqhd,bkhd->bhqk', qn, k_nope)
              + jnp.einsum('bqhr,bkr->bhqk', qp, k_pe)).astype(jnp.float32) * scale
        p = jax.nn.softmax(sc, axis=-1)
        return jnp.einsum('bhqk,bkhd->bqhd', p.astype(v.dtype), v)

    o = lax.map(block, (to_blocks(q_nope), to_blocks(q_pe)))
    return o.swapaxes(0, 1).reshape(b, s, WIDTH_B)

def hybrid_mixer(xn, positions, cos, sin, w_in, g_q_a, w_q_b, g_kv_a, w_kv_b,
                 rel_bias, g_out_a, g_out_b, w_o):
    b, s, _ = xn.shape
    z = xn @ w_in
    cuts = [WIDTH_A, 2 * WIDTH_A, 3 * WIDTH_A, 3 * WIDTH_A + Q_LORA_RANK,
            3 * WIDTH_A + Q_LORA_RANK + KV_LORA_RANK]
    qa, ka, va, zq, zkv, zkpe = jnp.split(z, cuts, axis=-1)
    shp_a = (b, s, N_HEADS_A, HEAD_DIM_A)
    o_a = dilated_attention(qa.reshape(shp_a), ka.reshape(shp_a), va.reshape(shp_a),
                            positions, rel_bias)
    q = (rmsnorm(zq, g_q_a) @ w_q_b).reshape(b, s, N_HEADS_B, QK_NOPE_DIM + QK_ROPE_DIM)
    q_nope, q_pe = jnp.split(q, [QK_NOPE_DIM], axis=-1)
    q_pe = apply_rope(q_pe, cos[:, :, None, :], sin[:, :, None, :])
    kv = (rmsnorm(zkv, g_kv_a) @ w_kv_b).reshape(b, s, N_HEADS_B, QK_NOPE_DIM + V_DIM_B)
    k_nope, v_b = jnp.split(kv, [QK_NOPE_DIM], axis=-1)
    k_pe = apply_rope(zkpe, cos, sin)
    o_b = mla_attention(q_nope, q_pe, k_nope, k_pe, v_b)
    o = jnp.concatenate([rmsnorm(o_a, g_out_a), rmsnorm(o_b, g_out_b)], axis=-1)
    return o @ w_o

def memory_cross_attention(hn, mem, g_mem, w_mq, w_mkv, w_mo):
    b, s, _ = hn.shape
    m = mem.shape[1]
    q = (hn @ w_mq).reshape(b, s, N_HEADS_MEM, HEAD_DIM_MEM)
    kv = (rmsnorm(mem, g_mem) @ w_mkv).reshape(b, m, 2, N_HEADS_MEM, HEAD_DIM_MEM)
    k, v = kv[:, :, 0], kv[:, :, 1]
    sc = jnp.einsum('bqhd,bmhd->bhqm', q, k).astype(jnp.float32) * HEAD_DIM_MEM ** -0.5
    p = jax.nn.softmax(sc, axis=-1)
    o = jnp.einsum('bhqm,bmhd->bqhd', p.astype(v.dtype), v).reshape(b, s, D_MODEL)
    return o @ w_mo

def moe_ffn(hn, w_router, b_router, w_gate_up, b_gate_up, w_down, b_down):
    b, s, d = hn.shape
    t = b * s
    xt = hn.reshape(t, d)
    logits = (xt @ w_router + b_router).astype(jnp.float32)
    top_val, top_idx = lax.top_k(logits, TOP_K)
    gates = jax.nn.softmax(top_val, axis=-1)
    n_assign = t * TOP_K
    flat_e = top_idx.reshape(-1)
    order = jnp.argsort(flat_e)
    sorted_e = flat_e[order]
    sorted_tok = (order // TOP_K).astype(jnp.int32)
    counts = jnp.bincount(flat_e, length=N_EXPERTS)
    padded = ((counts + EXPERT_BLOCK - 1) // EXPERT_BLOCK) * EXPERT_BLOCK
    ends = jnp.cumsum(padded)
    pad_start = ends - padded
    start = jnp.cumsum(counts) - counts
    dest = pad_start[sorted_e] + (jnp.arange(n_assign) - start[sorted_e])
    n_blk = -(-n_assign // EXPERT_BLOCK) + N_EXPERTS
    m_pad = n_blk * EXPERT_BLOCK
    tok_buf = jnp.zeros((m_pad,), jnp.int32).at[dest].set(sorted_tok)
    gate_buf = jnp.zeros((m_pad,), xt.dtype).at[dest].set(
        gates.reshape(-1)[order].astype(xt.dtype))
    block_expert = jnp.clip(
        jnp.searchsorted(ends, jnp.arange(n_blk) * EXPERT_BLOCK, side='right'),
        0, N_EXPERTS - 1)

    def expert_block(args):
        e, tok = args
        xb = xt[tok]
        gu = xb @ w_gate_up[e] + b_gate_up[e]
        gate, up = jnp.split(gu, 2, axis=-1)
        gate = jnp.minimum(gate, SWIGLU_LIMIT)
        up = jnp.clip(up, -SWIGLU_LIMIT, SWIGLU_LIMIT)
        hmid = (up + 1.0) * (gate * jax.nn.sigmoid(SWIGLU_ALPHA * gate))
        return hmid @ w_down[e] + b_down[e]

    out = lax.map(expert_block, (block_expert, tok_buf.reshape(n_blk, EXPERT_BLOCK)))
    out = out.reshape(m_pad, d) * gate_buf[:, None]
    y = jnp.zeros((t, d), xt.dtype).at[tok_buf].add(out)
    return y.reshape(b, s, d)

def setup_inputs(seed: int = 0) -> dict:
    key = jax.random.key(seed)
    ks = jax.random.split(key, 32)
    f32 = jnp.float32
    L = DEPTH

    def nrm(k, shape, scale):
        return jax.random.normal(k, shape, f32) * scale

    def gain(k, shape):
        return 1.0 + 0.05 * jax.random.normal(k, shape, f32)

    x = nrm(ks[0], (BATCH, SEQ, D_MODEL), 1.0)
    mem = nrm(ks[1], (BATCH, N_MEM, D_MODEL), 1.0)
    positions = (jnp.arange(SEQ, dtype=jnp.int32)[None, :]
                 + jax.random.randint(ks[2], (BATCH, 1), 0, 1024, dtype=jnp.int32))
    return {
        "x": x,
        "mem": mem,
        "positions": positions,
        "g_mix": gain(ks[3], (L, D_MODEL)),
        "w_in": nrm(ks[4], (L, D_MODEL, IN_PROJ_WIDTH), D_MODEL ** -0.5),
        "g_q_a": gain(ks[5], (L, Q_LORA_RANK)),
        "w_q_b": nrm(ks[6], (L, Q_LORA_RANK, N_HEADS_B * (QK_NOPE_DIM + QK_ROPE_DIM)), Q_LORA_RANK ** -0.5),
        "g_kv_a": gain(ks[7], (L, KV_LORA_RANK)),
        "w_kv_b": nrm(ks[8], (L, KV_LORA_RANK, N_HEADS_B * (QK_NOPE_DIM + V_DIM_B)), KV_LORA_RANK ** -0.5),
        "rel_bias": nrm(ks[9], (NUM_BUCKETS, N_HEADS_A), 0.5),
        "g_out_a": gain(ks[10], (L, WIDTH_A)),
        "g_out_b": gain(ks[11], (L, WIDTH_B)),
        "w_o": nrm(ks[12], (L, MIX_WIDTH, D_MODEL), MIX_WIDTH ** -0.5),
        "g_xattn": gain(ks[13], (L, D_MODEL)),
        "g_mem": gain(ks[14], (L, D_MODEL)),
        "w_mq": nrm(ks[15], (L, D_MODEL, D_MODEL), D_MODEL ** -0.5),
        "w_mkv": nrm(ks[16], (L, D_MODEL, 2 * D_MODEL), D_MODEL ** -0.5),
        "w_mo": nrm(ks[17], (L, D_MODEL, D_MODEL), D_MODEL ** -0.5),
        "g_moe": gain(ks[18], (L, D_MODEL)),
        "w_router": nrm(ks[19], (L, D_MODEL, N_EXPERTS), D_MODEL ** -0.5),
        "b_router": nrm(ks[20], (L, N_EXPERTS), 0.01),
        "w_gate_up": nrm(ks[21], (L, N_EXPERTS, D_MODEL, 2 * D_EXPERT), D_MODEL ** -0.5),
        "b_gate_up": nrm(ks[22], (L, N_EXPERTS, 2 * D_EXPERT), 0.02),
        "w_down": nrm(ks[23], (L, N_EXPERTS, D_EXPERT, D_MODEL), D_EXPERT ** -0.5),
        "b_down": nrm(ks[24], (L, N_EXPERTS, D_MODEL), 0.02),
        "g_final": gain(ks[25], (D_MODEL,)),
    }

def reference(x, mem, positions, g_mix, w_in, g_q_a, w_q_b, g_kv_a, w_kv_b, rel_bias,
              g_out_a, g_out_b, w_o, g_xattn, g_mem, w_mq, w_mkv, w_mo, g_moe,
              w_router, b_router, w_gate_up, b_gate_up, w_down, b_down, g_final):
    cos, sin = rope_cos_sin(positions)
    h = x
    for l in range(DEPTH):
        h = h + hybrid_mixer(rmsnorm(h, g_mix[l]), positions, cos, sin, w_in[l], g_q_a[l],
                             w_q_b[l], g_kv_a[l], w_kv_b[l], rel_bias, g_out_a[l],
                             g_out_b[l], w_o[l])
        h = h + memory_cross_attention(rmsnorm(h, g_xattn[l]), mem, g_mem[l], w_mq[l],
                                       w_mkv[l], w_mo[l])
        h = h + moe_ffn(rmsnorm(h, g_moe[l]), w_router[l], b_router[l], w_gate_up[l],
                        b_gate_up[l], w_down[l], b_down[l])
    return rmsnorm(h, g_final)


_drawn_inputs = setup_inputs


def setup_inputs(seed=0):
    import zlib

    import numpy as np

    out = dict(_drawn_inputs(seed))
    spreads = {}
    factors = {'g_xattn': 3.959, 'g_mem': 2.746, 'b_gate_up': 6.829, 'b_down': 7.861, 'b_router': 3.597}
    for name, (base, spread) in spreads.items():
        noise = np.random.default_rng([zlib.crc32(name.encode()), seed]).standard_normal(out[name].shape)
        drawn = base * np.exp(spread * noise) if base else spread * noise
        out[name] = __import__('jax').numpy.asarray(drawn.astype(out[name].dtype))
    for name, factor in factors.items():
        out[name] = (out[name] * factor).astype(out[name].dtype)
    return out
```

```python
import concourse.bass as bass
from concourse import mybir
from contextlib import ExitStack
import numpy as np

P = 128
D = 1024
SEQ = 256
TT = SEQ // P
KC = D // P
HEADS, DH = 8, 64
WA = HEADS * DH
QL, KVL = 256, 128
ROPE, NOPE = 32, 64
DQB = NOPE + ROPE
ZW = 3 * WA + QL + KVL + ROPE
ZN = ZW // 4
MH, MDH = 4, 256
NB = 32
NE, TOPK = 32, 4
BLK = 64
NOVF = SEQ * TOPK // BLK
NITEM = NE + NOVF
SLOT = 2048
NGU, NDN = 8, 4
NCH = NGU + NDN
EPS = 1e-6
BIG = 4096.0
LIMIT, ALPHA = 7.0, 1.702
PATTERNS = ((128, 1), (512, 4), (2048, 16))
LARGE = (8, 15, 27, 50, 91, 166, 305, 559)
FROM = list(range(8)) + list(LARGE)
ORDER = list(range(15, 0, -1)) + [0] + list(range(17, 32))
STEPS = [-1e9] + [1 - FROM[b + 1] for b in range(14, 0, -1)] + [0] + [FROM[b - 16] for b in range(17, 32)]

C_ID = 0
C_LOGM = C_ID + P
C_UP = C_LOGM + TT * SEQ
C_IOTA = C_UP + P
C_EXP = C_IOTA + P
C_STEP = C_EXP + NE
C_FREQ = C_STEP + 1
C_MOD = C_FREQ + ROPE // 2
C_ITEM = C_MOD + NE
C_END = C_ITEM + NOVF
G_MIX, G_X, G_MEM, G_MOE, G_OUT, G_QA, G_KVA = 0, 8, 16, 24, 32, 40, 42
G_END = 43


def shape_constants():
    c = np.zeros((P, C_END), np.float32)
    p = np.arange(P)
    c[:, C_ID:C_ID + P] = np.eye(P)
    for t in range(TT):
        off = np.arange(SEQ)[None, :] - (t * P + p)[:, None]
        n = sum(((off % d == 0) & (np.abs(off) <= w // 2)).astype(int) for w, d in PATTERNS)
        c[:, C_LOGM + t * SEQ:C_LOGM + (t + 1) * SEQ] = np.where(n > 0, np.log(np.maximum(n, 1)), -1e30)
    c[:, C_UP:C_UP + P] = p[:, None] < p[None, :]
    c[:, C_IOTA:C_IOTA + P] = p[None, :] % BLK
    c[:, C_EXP:C_EXP + NE] = np.arange(NE)[None, :]
    c[:, C_STEP] = (STEPS + [1e9])[0:NB] * (P // NB)
    c[:, C_FREQ:C_FREQ + ROPE // 2] = np.float32(10000.0) ** (-np.arange(0, ROPE, 2, dtype=np.float32) / ROPE)
    c[:, C_MOD:C_MOD + NE] = (p % NE)[:, None] == np.arange(NE)[None, :]
    c[:, C_ITEM:C_ITEM + NOVF] = np.arange(NOVF)[None, :]
    return c


def encoder_kernel(nc, x, mem, pos, pos_col, posk, consts, gains, w_in, w_q_b, w_kv_b, rel_cur, rel_prev, w_o,
                   w_mq, w_mkv, w_mo, w_router, b_router, w_gate_up, b_gate_up, w_down, b_down,
                   g_final, out):
    f32, bf16 = mybir.dt.float32, mybir.dt.bfloat16
    i32, u32 = mybir.dt.int32, mybir.dt.uint32
    ALU = mybir.AluOpType
    ACT = mybir.ActivationFunctionType
    X = mybir.AxisListType.X

    ctx = ExitStack()
    with ctx:
        def sb(name, cols, dt=f32):
            return ctx.enter_context(nc.sbuf_tensor(name, [P, cols], dt))

        ring = sb("ring", NCH * SLOT)
        stage = sb("stage", KC * ZW)
        h = sb("h", TT * D)[:, :].rearrange("p (t d) -> p t d", t=TT)
        kT_mem = sb("kT_mem", KC * SEQ)[:, :].rearrange("p (c m) -> p c m", c=KC)
        v_mem = sb("v_mem", TT * D)[:, :].rearrange("p (t d) -> p t d", t=TT)
        nT_flat = sb("nT", KC * SEQ)
        nT = nT_flat[:, :].rearrange("p (c m) -> p c m", c=KC)
        spare = sb("spare", TT * D)
        cst = sb("cst", C_END)
        gain = sb("gain", G_END)
        ones_bf = sb("ones_bf", P, bf16)
        up_bf = sb("up_bf", P, bf16)
        stat = sb("stat", 148)
        trig = sb("trig", 6 * 32)

        def in_ring(lo, n):
            return ring[:, lo:lo + n]

        def in_stage(lo, n):
            return stage[:, lo:lo + n]

        def spl(ap, t):
            return ap.rearrange("p (t d) -> p t d", t=t)

        def slot(c):
            return ring[:, c * SLOT:(c + 1) * SLOT]

        def over(ap, shape):
            return ap.to_broadcast(shape)

        ident = cst[:, C_ID:C_ID + P]
        iota = cst[:, C_IOTA:C_IOTA + P]
        win = spl(in_stage(0, KC * ZW), KC)
        wmkv = spl(in_ring(0, KC * 2 * D), KC)
        xn = spl(spare[:, :], TT)
        bias = in_ring(0, TT * HEADS * SEQ).rearrange("p (t h k) -> p t h k", t=TT, h=HEADS)
        qb = spl(in_ring(4096, TT * HEADS * DQB), TT)
        v_b = spl(in_ring(5632, TT * WA), TT)
        k96 = spl(in_ring(6656, TT * HEADS * DQB), TT)
        qT96 = spl(in_ring(8192, HEADS * SEQ), HEADS)
        kT96 = spl(in_ring(10240, HEADS * SEQ), HEADS)
        NL = 4
        logit = spl(in_ring(12288, NL * SEQ), NL)
        prob = spl(in_ring(13312, NL * SEQ), NL)
        probT = spl(in_ring(14336, NL * SEQ), NL)
        steps = in_ring(16384, 4096).bitcast(bf16).rearrange("p (k q) -> p k q", q=SEQ)
        wqb = spl(in_ring(20480, 2 * HEADS * DQB), 2)
        wkvb = in_ring(22016, HEADS * (NOPE + DH))
        zn = spl(in_ring(23040, TT * (QL + KVL)), TT)
        znT = spl(in_ring(23808, 3 * SEQ), 3)
        qT_a = spl(spare[:, 0:4 * SEQ], 4)
        kT_a = spl(spare[:, 4 * SEQ:8 * SEQ], 4)
        z = spl(in_stage(8192, TT * ZW), TT)
        o_cat = spl(in_stage(12096, TT * D), TT)
        rope_t = in_stage(14144, 4 * HEADS * ROPE // 2)
        w_sq = spl(in_stage(0, KC * D), KC)
        wmq = spl(in_ring(NGU * SLOT, KC * D), KC)
        qT_m = spl(in_stage(8192, KC * SEQ), KC)
        bgu_raw = in_stage(10240, 2 * D)
        prob_m = spl(in_stage(12288, NL * SEQ), NL)
        probT_m = in_stage(13312, 2 * TT * SEQ).rearrange("p (j m q) -> p j m q", j=2, m=TT)
        wr = spl(in_stage(14336, KC * NE), KC)
        bdn = in_stage(14592, D)
        oT_m = spl(spare[:, :], KC)
        part = [in_stage(i * D, D).bitcast(bf16).rearrange("p (t d) -> p t d", t=TT) for i in range(3)]
        rest = spl(in_stage(3072, TT * D), TT)
        xgT = in_stage(5120, 512)
        gate_s, up_s, sig_s, h_s = (in_stage(5632 + 512 * i, 512) for i in range(4))
        hT = in_stage(7680, 512)
        o_s = in_stage(8192, 512)
        gsel = in_stage(8704, TT * P)
        gtok = spl(in_stage(8960, TT * P), TT)
        bgu = in_stage(9216, D).bitcast(bf16)
        pick = spl(in_stage(12288, TT * BLK // 2).bitcast(bf16), TT)
        bsel = in_stage(12352, BLK // 2).bitcast(bf16)
        rt = in_stage(12384, 1152)
        gT = in_stage(13536, SEQ)
        own, val = (spl(nT_flat[:, i * NOVF * NE:(i + 1) * NOVF * NE], NOVF) for i in range(2))
        g_row = kT_mem[:, 0:4, :]

        bank = [ctx.enter_context(nc.psum_tensor(f"bank{i}", [P, 512], f32)) for i in range(8)]

        names = """
            ld_x ld_mem ld_cst ld_small ld_lora ld_wo ld_wmo ld_wr ld_late ld_row st_out vec_chain act_chain
            x_sq xn_ready xT_mm xT_ready z_mm z_act z_vec mem_sq memn_ready mT_mm mT_ready kT_mm kT_ready
            v_mm v_ready z_sq zn_ready zT_mm zT_ready qb_mm qb_ready kvb_mm kvb_ready steps_ready bias_mm
            bias_ev aT_mm qTa_ready kTa_ready ropek_ready q96_mm q96_ready k96_mm k96_ready
            s_mm s_read e_ready pT_mm pT_ready pv_mm o_ready o_sq on_ready oT_mm oT_ready wo_mm h_ready
            h_sq hn_ready hT_mm hTs_ready qm_mm qm_ready sm_mm em_ready pm_ready pmT_mm pmT_ready
            om_mm om_ready wm_mm h2_ready h2_sq h3_ready h3T_mm h3T_ready rt_mm split_act split_vec
            mask_ready rank_mm gate_e gates_ready gtT_mm gtT_ready y_init counts_ready ones_ready
            chunks_used gathered xg_ready scattered hid_mm hid_ready out_copied gsel_mm gsel_ready
            pick_ready bsel_ready gtok_ready gate_ready sig_ready up_ready gu_ready hmid_ready
            y_done f_ready f_sq fin_ready lnv newton mlnv znlnv onlnv hlnv h2lnv flnv trig_in sin_ready
        """.split()
        S = {n: ctx.enter_context(nc.semaphore(n)) for n in names}
        ld_win = [ctx.enter_context(nc.semaphore(f"ld_win{k}")) for k in range(KC)]
        ld_wmkv = [ctx.enter_context(nc.semaphore(f"ld_wmkv{k}")) for k in range(KC)]
        ld_wmq = [ctx.enter_context(nc.semaphore(f"ld_wmq{k}")) for k in range(NDN)]
        ld_exp = [ctx.enter_context(nc.semaphore(f"ld_exp{c}")) for c in range(NCH)]

        def rt2(lo, n):
            return rt[:, lo:lo + TT * n].rearrange("p (t n) -> p t n", t=TT)
        lg = rt2(0, NE)
        top = rt2(64, 8)
        topi = rt[:, 80:96].bitcast(u32).rearrange("p (t n) -> p t n", t=TT)
        topf = rt2(96, 8)
        eg = rt2(112, TOPK)
        oh = [rt[:, 128 + i * TOPK * NE:128 + (i + 1) * TOPK * NE].rearrange("p (j e) -> p j e", j=TOPK)
              for i in range(TT)]
        mask = rt2(384, NE)
        mask_bf = rt[:, 448:448 + NE].bitcast(bf16).rearrange("p (t n) -> p t n", t=TT)
        place = rt2(480, NITEM)
        gates = rt2(576, NITEM)
        onehot = rt[:, 672:672 + NITEM]
        cnt, extra, cum, cum2, beg = (rt[:, 720 + 32 * i:720 + 32 * (i + 1)] for i in range(5))
        items_i = rt[:, 944:945].bitcast(i32)
        novf_i = rt[:, 945:946].bitcast(i32)
        eid_f = rt[:, 948:948 + NOVF]
        eid_i = rt[:, 964:964 + NOVF].bitcast(i32)
        nmax0, esum, ersum = rt[:, 980:982], rt[:, 984:986], rt[:, 988:990]

        def st(lo, n):
            return stat[:, lo:lo + n]
        ss_x, ss_m, ss_z, ss_o, ss_h, ss_h2, ss_f = st(0, 2), st(2, 2), st(4, 4), st(8, 4), st(12, 2), st(14, 2), st(16, 2)
        rs_x, rs_m, rs_z, rs_o, rs_h, rs_h2, rs_f = st(20, 2), st(22, 2), st(24, 4), st(28, 4), st(32, 2), st(34, 2), st(36, 2)
        ms = st(40, 4)
        y0 = st(44, 4)
        nwt = st(48, 4)
        NU = 2 * HEADS * TT
        nmax, den = st(52, NU), st(84, NU)
        rden = st(116, NU)
        brow = trig[:, 160:192]
        poscol, posrow = sb("poscol", TT), sb("posrow", SEQ)
        poscol_i, posrow_i = sb("poscol_i", TT, i32), sb("posrow_i", SEQ, i32)
        posk_i, posk_f = sb("posk_i", SEQ // 4, i32), sb("posk_f", SEQ // 4)
        relc, relp = sb("relc", HEADS), sb("relp", HEADS)
        delta = sb("delta", HEADS * 3, bf16)[:, :].rearrange("p (h s) -> p h s", s=3)
        nm8, dn8, rd8 = sb("nm8", 8), sb("dn8", 8), sb("rd8", 8)

        block = ctx.enter_context(nc.Block())

        @block.sync
        def _(sp):
            sp.dma_start(h, x.rearrange("(t p) d -> p t d", p=P)).then_inc(S["ld_x"], 16)
            sp.dma_start(cst[:, :], consts).then_inc(S["ld_cst"], 16)
            sp.dma_start(gain[:, :], gains).then_inc(S["ld_cst"], 16)
            for k in range(KC):
                sp.dma_start(win[:, k, :], w_in[k * P:(k + 1) * P, :]).then_inc(ld_win[k], 16)
            sp.dma_start(v_mem, mem.rearrange("(t p) d -> p t d", p=P)).then_inc(S["ld_mem"], 16)
            sp.dma_start(wqb, w_q_b.rearrange("(c p) n -> p c n", p=P)).then_inc(S["ld_lora"], 16)
            sp.dma_start(wkvb, w_kv_b).then_inc(S["ld_lora"], 16)
            for k in range(KC):
                sp.dma_start(wmkv[:, k, :], w_mkv[k * P:(k + 1) * P, :]).then_inc(ld_wmkv[k], 16)
            sp.wait_ge(S["z_mm"], 8)
            sp.dma_start(w_sq, w_o.rearrange("(c p) n -> p c n", p=P)).then_inc(S["ld_wo"], 16)
            sp.wait_ge(S["pv_mm"], NU)
            for j in range(NDN):
                sp.dma_start(wmq[:, 2 * j:2 * j + 2, :],
                             w_mq[2 * j * P:(2 * j + 2) * P, :].rearrange("(c p) n -> p c n", p=P))\
                    .then_inc(ld_wmq[j], 16)
            sp.wait_ge(S["wo_mm"], 4)
            sp.dma_start(w_sq, w_mo.rearrange("(c p) n -> p c n", p=P)).then_inc(S["ld_wmo"], 16)
            sp.dma_start(wr, w_router.rearrange("(c p) n -> p c n", p=P)).then_inc(S["ld_wr"], 16)
            sp.dma_start(bdn[0:NE, :], b_down).then_inc(S["ld_late"], 16)
            for j in range(3):
                sp.dma_start(bgu_raw[NE * j:NE * (j + 1), :], b_gate_up).then_inc(S["ld_late"], 16)

            def load_chunk(c, e):
                if c < NGU:
                    sp.dma_start(slot(c), w_gate_up[e, c * P:(c + 1) * P, :]).then_inc(ld_exp[c], 16)
                else:
                    f = 2 * (c - NGU) * P
                    sp.dma_start(spl(slot(c), 2), w_down[e, f:f + 2 * P, :].rearrange("(j p) n -> p j n", p=P))\
                        .then_inc(ld_exp[c], 16)

            for c in range(NGU):
                load_chunk(c, 0)
            sp.wait_ge(S["qm_mm"], 4)
            for c in range(NGU, NCH):
                load_chunk(c, 0)
            sp.wait_ge(S["sm_mm"], MH * TT)
            sp.dma_start(g_row, g_final.rearrange("(a c n) -> a c n", a=1, c=4).to_broadcast([P, 4, SEQ])).then_inc(S["ld_row"], 16)
            wgu = w_gate_up.rearrange("e (c p) n -> c p e n", p=P)
            wdn = w_down.rearrange("e (c j p) n -> c p e j n", j=2, p=P)

            def load_next(c, e, used):
                sp.wait_ge(S["chunks_used"], used)
                if c < NGU:
                    sp.dma_start(slot(c), wgu[c, :, bass.ds(e, 1), :]).then_inc(ld_exp[c], 16)
                else:
                    sp.dma_start(spl(slot(c), 2), wdn[c - NGU, :, bass.ds(e, 1), :, :]).then_inc(ld_exp[c], 16)

            with sp.Fori(1, NE) as e:
                for c in range(NCH):
                    load_next(c, e, e * NCH + (c + 1 - NCH))
            sp.wait_ge(S["counts_ready"], 1)
            n_over = sp.value_load(novf_i[0:1, :], min_val=0, max_val=NOVF - 1)
            with sp.If(n_over > 0):
                with sp.Fori(0, n_over) as i:
                    e = sp.value_load(eid_i[0:1, bass.ds(i, 1)], min_val=0, max_val=NE - 1)
                    for c in range(NCH):
                        load_next(c, e, i * NCH + (c + 1 + (NE - 1) * NCH))
            for t in range(TT):
                sp.wait_ge(S["fin_ready"], t + 1)
                sp.dma_start(out[t * P:(t + 1) * P, :], h[:, t, :]).then_inc(S["st_out"], 16)
            sp.wait_ge(S["st_out"], 16 * TT)

        @block.scalar
        def _(act):
            act.dma_start(poscol_i[:, :], pos_col).then_inc(S["ld_small"], 16)
            act.dma_start(posrow_i[:, :], pos.rearrange("(a n) -> a n", a=1).to_broadcast([P, SEQ])).then_inc(S["ld_small"], 16)
            act.dma_start(posk_i[:, :], posk).then_inc(S["ld_small"], 16)
            act.dma_start(relc[:, :], rel_cur).then_inc(S["ld_small"], 16)
            act.dma_start(relp[:, :], rel_prev).then_inc(S["ld_small"], 16)
            act.dma_start(brow, b_router.rearrange("(a n) -> a n", a=1).to_broadcast([P, NE])).then_inc(S["ld_small"], 16)

            def inv_root(src, dst, ready, done):
                act.wait_ge(ready, 1)
                act.activation(dst, src, ACT.Ln).then_inc(S["act_chain"], 1)
                act_links[0] += 1
                act.wait_ge(S["act_chain"], act_links[0])
                act.activation(dst, dst, ACT.Exp, scale=-0.5).then_inc(done, 1)
            act_links = [0]

            act.wait_ge(S["ld_x"], 16)
            for t in range(TT):
                act.activation(xn[:, t, :], h[:, t, :], ACT.Square, accum_out=ss_x[:, t:t + 1]).then_inc(S["x_sq"], 1)
            inv_root(ms[:, 0:2], y0[:, 0:2], S["lnv"], S["newton"])
            act.wait_ge(S["ld_mem"], 16)
            for t in range(TT):
                act.activation(kT_mem[:, 4 * t:4 * t + 4, :], v_mem[:, t, :].rearrange("p (c m) -> p c m", c=4),
                               ACT.Square, accum_out=ss_m[:, t:t + 1]).then_inc(S["mem_sq"], 1)
            inv_root(ms[:, 0:2], y0[:, 0:2], S["mlnv"], S["newton"])
            act.wait_ge(S["trig_in"], 1)
            act.activation(trig[:, 0:64], trig[:, 64:128], ACT.Sin).then_inc(S["sin_ready"], 1)
            for i in range(0, 8, 2):
                act.wait_ge(S["z_mm"], i + 1)
                if i == 0:
                    act.wait_ge(S["z_mm"], 8)
                act.activation(z[:, i // 4, (i % 4) * ZN:(i % 4 + 1) * ZN], bank[i][:, 0:ZN], ACT.Copy).then_inc(S["z_act"], 1)
            act.wait_ge(S["z_act"], 4)
            act.wait_ge(S["z_vec"], 4)
            for t in range(TT):
                act.activation(zn[:, t, 0:QL], z[:, t, 3 * WA:3 * WA + QL], ACT.Square,
                               accum_out=ss_z[:, t:t + 1]).then_inc(S["z_sq"], 1)
                act.activation(zn[:, t, QL:QL + KVL], z[:, t, 3 * WA + QL:3 * WA + QL + KVL], ACT.Square,
                               accum_out=ss_z[:, 2 + t:3 + t]).then_inc(S["z_sq"], 1)
            inv_root(ms[:, 0:4], y0[:, 0:4], S["znlnv"], S["newton"])
            for j in range(4):
                act.wait_ge(S["kT_mm"], j + 1)
                act.activation(kT_mem[:, 2 * j:2 * j + 2, :], spl(bank[4 + j][:, :], 2), ACT.Copy).then_inc(S["kT_ready"], 1)
            for j in range(4):
                act.wait_ge(S["v_mm"], j + 1)
                t, n = divmod(j, 2)
                act.activation(v_mem[:, t, n * 512:(n + 1) * 512], bank[j][:, :], ACT.Copy).then_inc(S["v_ready"], 1)
            for j in range(4):
                act.wait_ge(S["qb_mm"], j + 1)
                t, n = divmod(j, 2)
                act.activation(qb[:, t, n * 384:(n + 1) * 384], bank[j][:, 0:384], ACT.Copy).then_inc(S["qb_ready"], 1)
            for j in range(2):
                act.wait_ge(S["aT_mm"], j + 1)
                act.activation(qT_a[:, 2 * j:2 * j + 2, :], spl(bank[4 + j][:, :], 2), ACT.Copy,
                               scale=DH ** -0.5).then_inc(S["qTa_ready"], 1)
            for j in range(4):
                act.wait_ge(S["q96_mm"], j + 1)
                act.activation(qT96[0:DQB, 2 * j:2 * j + 2, :], spl(bank[4 + j][0:DQB, :], 2), ACT.Copy,
                               scale=DQB ** -0.5).then_inc(S["q96_ready"], 1)
            for j in range(4):
                act.wait_ge(S["k96_mm"], j + 1)
                act.activation(kT96[0:DQB, 2 * j:2 * j + 2, :], spl(bank[4 + j][0:DQB, :], 2), ACT.Copy).then_inc(S["k96_ready"], 1)

            def transposed(u):
                act.wait_ge(S["pT_mm"], u + 1)
                if u >= NL:
                    act.wait_ge(S["pv_mm"], u - NL + 1)
                act.activation(probT[:, u % NL, :], bank[(2, 7)[u % 2]][:, 0:SEQ], ACT.Copy).then_inc(S["pT_ready"], 1)

            for u in range(NU):
                act.wait_ge(S["s_read"], u + 1)
                if u >= NL:
                    act.wait_ge(S["pT_mm"], u - NL + 1)
                src = logit[:, u % NL, :] if u < NU // 2 else bank[u % 2][:, 0:SEQ]
                act.activation(prob[:, u % NL, :], src, ACT.Exp, bias=nmax[:, u:u + 1],
                               accum_out=den[:, u:u + 1]).then_inc(S["e_ready"], 1)
                if u >= 2:
                    transposed(u - 2)
            transposed(NU - 2)
            transposed(NU - 1)
            for t in range(TT):
                act.wait_ge(S["o_ready"], 4 if t else 3)
                for a in range(2):
                    act.activation(nT[:, 4 * t + 2 * a:4 * t + 2 * a + 2, :],
                                   o_cat[:, t, a * WA:(a + 1) * WA].rearrange("p (c m) -> p c m", c=2), ACT.Square,
                                   accum_out=ss_o[:, 2 * t + a:2 * t + a + 1]).then_inc(S["o_sq"], 1)
            inv_root(ms[:, 0:4], y0[:, 0:4], S["onlnv"], S["newton"])
            for t in range(TT):
                act.wait_ge(S["h_ready"], 2 * t + 2)
                act.activation(xn[:, t, :], h[:, t, :], ACT.Square, accum_out=ss_h[:, t:t + 1]).then_inc(S["h_sq"], 1)
            inv_root(ms[:, 0:2], y0[:, 0:2], S["hlnv"], S["newton"])
            for j in range(4):
                act.wait_ge(S["qm_mm"], j + 1)
                act.activation(qT_m[:, 2 * j:2 * j + 2, :], spl(bank[4 + j][:, :], 2), ACT.Copy,
                               scale=MDH ** -0.5).then_inc(S["qm_ready"], 1)
            for u in range(MH * TT):
                act.wait_ge(S["pm_ready"], 2 * u + 1)
                if u >= NL:
                    act.wait_ge(S["pmT_mm"], (u - NL) // TT + 1)
                act.activation(prob_m[:, u % NL, :], bank[u % 2][:, 0:SEQ], ACT.Exp, bias=nm8[:, u:u + 1],
                               accum_out=dn8[:, u:u + 1]).then_inc(S["em_ready"], 1)
                if u % TT == 1 and u >= 3:
                    hd = u // TT - 1
                    act.wait_ge(S["pmT_mm"], hd + 1)
                    if hd >= 2:
                        act.wait_ge(S["om_mm"], hd - 1)
                    act.activation(probT_m[:, hd % 2, :, :], spl(bank[2 + hd % 2][:, :], 2), ACT.Copy).then_inc(S["pmT_ready"], 1)
            hd = MH - 1
            act.wait_ge(S["pmT_mm"], hd + 1)
            act.wait_ge(S["om_mm"], hd - 1)
            act.activation(probT_m[:, hd % 2, :, :], spl(bank[2 + hd % 2][:, :], 2), ACT.Copy).then_inc(S["pmT_ready"], 1)
            for hd in range(MH):
                act.wait_ge(S["om_mm"], hd + 1)
                act.activation(oT_m[:, 2 * hd:2 * hd + 2, :], spl(bank[4 + hd % 2][:, :], 2), ACT.Copy).then_inc(S["om_ready"], 1)
            for t in range(TT):
                act.wait_ge(S["h2_ready"], 2 * t + 2)
                act.activation(nT_flat[:, t * D:(t + 1) * D], h[:, t, :], ACT.Square, accum_out=ss_h2[:, t:t + 1])\
                    .then_inc(S["h2_sq"], 1)
            inv_root(ms[:, 0:2], y0[:, 0:2], S["h2lnv"], S["newton"])
            act.wait_ge(S["h3_ready"], 2)
            for j in range(3):
                if j:
                    act.wait_ge(S["split_vec"], j)
                act.activation(part[j], (rest if j else xn), ACT.Copy).then_inc(S["split_act"], 1)
            act.wait_ge(S["gate_e"], 1)
            for t in range(TT):
                act.activation(eg[:, t, :], top[:, t, 0:TOPK], ACT.Exp, bias=nmax0[:, t:t + 1],
                               accum_out=esum[:, t:t + 1]).then_inc(S["gate_e"], 1)
            act.wait_ge(S["counts_ready"], 1)
            items = act.value_load(items_i[0:1, :], min_val=NE, max_val=NITEM - 1)
            with act.Fori(0, items) as w:
                act.wait_ge(S["gate_ready"], w + 1)
                act.activation(sig_s, gate_s, ACT.Sigmoid, scale=ALPHA).then_inc(S["sig_ready"], 1)
                act.wait_ge(S["hid_mm"], w + 1)
                act.activation(hT, bank[2][:, :], ACT.Copy).then_inc(S["hid_ready"], 1)
                act.wait_ge(S["chunks_used"], w * NCH + NCH)
                act.wait_ge(S["scattered"], w + 1)
                act.activation(o_s, bank[3][:, :], ACT.Copy).then_inc(S["out_copied"], 1)
                act.wait_ge(S["gsel_mm"], w + 1)
                act.activation(gsel, bank[2][:, 0:TT * P], ACT.Copy).then_inc(S["gsel_ready"], 1)
            for t in range(TT):
                act.wait_ge(S["f_ready"], 2 * t + 2)
                act.activation(xn[:, t, :], h[:, t, :], ACT.Square, accum_out=ss_f[:, t:t + 1]).then_inc(S["f_sq"], 1)
            inv_root(ms[:, 0:2], y0[:, 0:2], S["flnv"], S["newton"])

        @block.vector
        def _(dve):
            links = [0]

            def link(ins):
                links[0] += 1
                ins.then_inc(S["vec_chain"], 1)
                dve.wait_ge(S["vec_chain"], links[0])

            newtons = [0]

            def mean_square(ss, n, width, ready):
                link(dve.tensor_scalar(nwt[:, 0:n], ss, 1.0 / width, EPS, ALU.mult, ALU.add))
                dve.tensor_copy(ms[:, 0:n], nwt[:, 0:n]).then_inc(ready, 1)

            def refine(rs, n, steps_before=0):
                newtons[0] += 1 + steps_before
                dve.wait_ge(S["newton"], newtons[0])
                link(dve.tensor_tensor(nwt[:, 0:n], ms[:, 0:n], y0[:, 0:n], ALU.mult))
                link(dve.tensor_tensor(nwt[:, 0:n], nwt[:, 0:n], y0[:, 0:n], ALU.mult))
                link(dve.tensor_scalar(nwt[:, 0:n], nwt[:, 0:n], -0.5, 1.5, ALU.mult, ALU.add))
                link(dve.tensor_tensor(rs, nwt[:, 0:n], y0[:, 0:n], ALU.mult))

            def with_gain(dst, src, col, n, m):
                return dve.tensor_tensor(dst, src, over(gain[:, col:col + n].unsqueeze(2), [P, n, m]), ALU.mult)

            def gained(mm, ready, col, first_bank, per=4):
                for i in range(4):
                    t, b = divmod(i, 2)
                    dve.wait_ge(mm, i + 1)
                    with_gain(nT[:, 4 * b:4 * b + 4, t * P:(t + 1) * P], spl(bank[first_bank + i][:, :], 4),
                              col + 4 * b, 4, P).then_inc(ready, 1)

            dve.wait_ge(S["x_sq"], 2)
            mean_square(ss_x, 2, D, S["lnv"])
            refine(rs_x, 2)
            for t in range(TT):
                dve.tensor_scalar(xn[:, t, :], h[:, t, :], rs_x[:, t:t + 1], None, ALU.mult).then_inc(S["xn_ready"], 1)
            dve.wait_ge(S["ld_cst"], 32)
            gained(S["xT_mm"], S["xT_ready"], G_MIX, 0)
            dve.wait_ge(S["mem_sq"], 2)
            mean_square(ss_m, 2, D, S["mlnv"])
            refine(rs_m, 2)
            for t in range(TT):
                dve.tensor_scalar(v_mem[:, t, :], v_mem[:, t, :], rs_m[:, t:t + 1], None, ALU.mult).then_inc(S["memn_ready"], 1)
            dve.wait_ge(S["ld_small"], 96)
            dve.tensor_copy(poscol[:, :], poscol_i[:, :]).then_inc(S["vec_chain"], 1)
            dve.tensor_copy(posrow[:, :], posrow_i[:, :]).then_inc(S["vec_chain"], 1)
            links[0] += 2
            link(dve.tensor_copy(posk_f[:, :], posk_i[:, :]))
            ang, red, cnt_t = trig[:, 64:96], trig[:, 96:128], trig[:, 128:160]
            half = ROPE // 2
            for t in range(TT):
                link(dve.tensor_scalar(ang[:, t * half:(t + 1) * half], cst[:, C_FREQ:C_FREQ + half],
                                       poscol[:, t:t + 1], None, ALU.mult))
            magic = 12582912.0
            link(dve.tensor_scalar(cnt_t, ang, float(1 / (2 * np.pi)), magic, ALU.mult, ALU.add))
            link(dve.tensor_scalar(cnt_t, cnt_t, -magic, None, ALU.add))
            c1 = 6.28125
            c2 = float(np.float32(np.round((2 * np.pi - c1) * 2 ** 21) / 2 ** 21))
            c3 = float(2 * np.pi - c1 - c2)
            for c in (c1, c2, c3):
                link(dve.scalar_tensor_tensor(ang, cnt_t, -c, ang, ALU.mult, ALU.add))
            link(dve.tensor_scalar(ang, ang, 3.1415925, -3.1415925, ALU.min, ALU.max))
            link(dve.tensor_scalar(red, ang, -1.0, None, ALU.mult))
            link(dve.tensor_tensor(red, red, ang, ALU.max))
            dve.tensor_scalar(red, red, -1.0, float(np.pi / 2), ALU.mult, ALU.add).then_inc(S["trig_in"], 1)
            link(dve.tensor_tensor(relc[:, :], relc[:, :], relp[:, :], ALU.subtract))
            for j in range(3):
                link(dve.tensor_copy(delta[:, :, j], relc[:, :]))
                if j < 2:
                    link(dve.tensor_tensor(relc[:, :], relc[:, :], delta[:, :, j], ALU.subtract))
            link(dve.memset(ones_bf[:, :], 1.0))
            dve.tensor_copy(up_bf[:, :], cst[:, C_UP:C_UP + P]).then_inc(S["ones_ready"], 1)
            for i in range(1, 8, 2):
                dve.wait_ge(S["z_mm"], i + 1)
                if i == 1:
                    dve.wait_ge(S["z_mm"], 8)
                dve.tensor_copy(z[:, i // 4, (i % 4) * ZN:(i % 4 + 1) * ZN], bank[i][:, 0:ZN]).then_inc(S["z_vec"], 1)
            gained(S["mT_mm"], S["mT_ready"], G_MEM, 0)

            dve.wait_ge(S["z_sq"], 4)
            link(dve.tensor_scalar(nwt[:, 0:2], ss_z[:, 0:2], 1.0 / QL, EPS, ALU.mult, ALU.add))
            link(dve.tensor_scalar(nwt[:, 2:4], ss_z[:, 2:4], 1.0 / KVL, EPS, ALU.mult, ALU.add))
            dve.tensor_copy(ms[:, 0:4], nwt[:, 0:4]).then_inc(S["znlnv"], 1)
            refine(rs_z, 4)
            for t in range(TT):
                dve.tensor_scalar(zn[:, t, 0:QL], z[:, t, 3 * WA:3 * WA + QL], rs_z[:, t:t + 1], None,
                                  ALU.mult).then_inc(S["zn_ready"], 1)
                dve.tensor_scalar(zn[:, t, QL:QL + KVL], z[:, t, 3 * WA + QL:3 * WA + QL + KVL],
                                  rs_z[:, 2 + t:3 + t], None, ALU.mult).then_inc(S["zn_ready"], 1)

            def bucket_steps(half_no):
                n = SEQ // 8
                keys = posk_f[:, half_no * n:(half_no + 1) * n]
                dve.scalar_tensor_tensor(steps, over(keys.unsqueeze(2), [P, n, SEQ]), cst[:, C_STEP:C_STEP + 1],
                                         over(posrow[:, :].unsqueeze(1), [P, n, SEQ]), ALU.subtract,
                                         ALU.is_ge).then_inc(S["steps_ready"], 1)

            bucket_steps(0)
            dve.wait_ge(S["zT_mm"], 1)
            with_gain(znT[:, 0:2, :], spl(bank[4][:, :], 2), G_QA, 2, SEQ).then_inc(S["zT_ready"], 1)
            with_gain(znT[:, 2:3, :], spl(bank[5][:, 0:SEQ], 1), G_KVA, 1, SEQ).then_inc(S["zT_ready"], 1)
            for j in range(4):
                t, n = divmod(j, 2)
                dve.wait_ge(S["kvb_mm"], j + 1)
                src = bank[4 + j][:, :].rearrange("p (h n) -> p h n", h=4)
                kd = k96[:, t, :].rearrange("p (h n) -> p h n", h=HEADS)
                vd = v_b[:, t, :].rearrange("p (h n) -> p h n", h=HEADS)
                dve.tensor_copy(kd[:, 4 * n:4 * n + 4, 0:NOPE], src[:, :, 0:NOPE])
                dve.tensor_copy(vd[:, 4 * n:4 * n + 4, :], src[:, :, NOPE:NOPE + DH]).then_inc(S["kvb_ready"], 1)
            dve.wait_ge(S["sin_ready"], 1)
            sin_c, cos_c = trig[:, 0:32], trig[:, 32:64]
            dve.wait_ge(S["qb_ready"], 4)
            for t in range(TT):
                qh = qb[:, t, :].rearrange("p (h n) -> p h n", h=HEADS)
                kz = z[:, t, ZW - ROPE:ZW].unsqueeze(1)
                kd = k96[:, t, :].rearrange("p (h n) -> p h n", h=HEADS)
                for src, nh, base in ((qh, HEADS, NOPE), (kz, 1, 0)):
                    a, b = src[:, :, base:base + half], src[:, :, base + half:base + ROPE]
                    cb = over(cos_c[:, t * half:(t + 1) * half].unsqueeze(1), [P, nh, half])
                    sbc = over(sin_c[:, t * half:(t + 1) * half].unsqueeze(1), [P, nh, half])
                    tm = [rope_t[:, i * 128:i * 128 + nh * half].rearrange("p (h n) -> p h n", h=nh) for i in range(4)]
                    dve.tensor_tensor(tm[0], a, cb, ALU.mult)
                    dve.tensor_tensor(tm[1], b, sbc, ALU.mult)
                    dve.tensor_tensor(tm[2], a, sbc, ALU.mult)
                    link(dve.tensor_tensor(tm[3], b, cb, ALU.mult))
                    if nh > 1:
                        dve.tensor_tensor(a, tm[0], tm[1], ALU.subtract)
                        link(dve.tensor_tensor(b, tm[2], tm[3], ALU.add))
                    else:
                        full = [P, HEADS, half]
                        dve.tensor_tensor(kd[:, :, NOPE:NOPE + half], over(tm[0], full), over(tm[1], full), ALU.subtract)
                        dve.tensor_tensor(kd[:, :, NOPE + half:DQB], over(tm[2], full), over(tm[3], full),
                                          ALU.add).then_inc(S["ropek_ready"], 1)
                        dve.wait_ge(S["ropek_ready"], t + 1)
            for j in range(2):
                dve.wait_ge(S["aT_mm"], 3 + j)
                dve.tensor_copy(kT_a[:, 2 * j:2 * j + 2, :], spl(bank[6 + j][:, :], 2)).then_inc(S["kTa_ready"], 1)

            def bias_out(f):
                hf, t, g, s = f // 16, f // 8 % 2, f // 2 % 4, f % 2
                dve.wait_ge(S["bias_mm"], f + 1)
                k0 = g * 64 + hf * 32 + s * 16
                dve.tensor_reduce(bias[:, t, :, k0:k0 + 16].rearrange("p h k -> p k h"),
                                  bank[f % 4][:, 0:384].rearrange("p (k h s) -> p k h s", k=16, s=3), X,
                                  ALU.add).then_inc(S["bias_ev"], 1)

            for f in range(16):
                bias_out(f)
            dve.wait_ge(S["bias_mm"], 16)
            bucket_steps(1)
            for f in range(16, 32):
                bias_out(f)
            dve.wait_ge(S["bias_ev"], 32)
            for t in range(TT):
                link(dve.tensor_tensor(bias[:, t, :, :], bias[:, t, :, :],
                                       over(cst[:, C_LOGM + t * SEQ:C_LOGM + (t + 1) * SEQ].unsqueeze(1),
                                            [P, HEADS, SEQ]), ALU.add))

            def attention_out(a):
                for t in range(TT):
                    dve.wait_ge(S["pv_mm"], a * 16 + 15 + t)
                    dd = den[:, a * 16:(a + 1) * 16].rearrange("p (h t) -> p t h", t=TT)
                    rr = rden[:, a * 16 + 8 * t:a * 16 + 8 * t + 8]
                    dve.wait_ge(S["e_ready"], (a + 1) * 16)
                    link(dve.reciprocal(rr, dd[:, t, :]))
                    dve.tensor_tensor(o_cat[:, t, a * WA:(a + 1) * WA].rearrange("p (h n) -> p h n", h=HEADS),
                                      bank[3 + 2 * a + t][:, :].rearrange("p (h n) -> p h n", h=HEADS),
                                      over(rr.unsqueeze(2), [P, HEADS, DH]), ALU.mult).then_inc(S["o_ready"], 1)

            for u in range(NU):
                hd, t = u % 16 // TT, u % TT
                dve.wait_ge(S["s_mm"], u + 1)
                if u < NU // 2:
                    if u >= NL:
                        dve.wait_ge(S["e_ready"], u - NL + 1)
                    dve.tensor_tensor(logit[:, u % NL, :], bank[u % 2][:, 0:SEQ], bias[:, t, hd, :],
                                      ALU.add).then_inc(S["vec_chain"], 1)
                    links[0] += 1
                    dve.wait_ge(S["vec_chain"], links[0])
                    dve.tensor_reduce(nmax[:, u:u + 1], logit[:, u % NL, :], X, ALU.max, negate=True).then_inc(S["s_read"], 1)
                else:
                    dve.tensor_reduce(nmax[:, u:u + 1], bank[u % 2][:, 0:SEQ], X, ALU.max, negate=True).then_inc(S["s_read"], 1)
                if u == NU // 2 + 4:
                    attention_out(0)
            attention_out(1)
            dve.wait_ge(S["o_sq"], 4)
            mean_square(ss_o, 4, WA, S["onlnv"])
            refine(rs_o, 4)
            for t in range(TT):
                for a in range(2):
                    dve.tensor_scalar(o_cat[:, t, a * WA:(a + 1) * WA], o_cat[:, t, a * WA:(a + 1) * WA],
                                      rs_o[:, 2 * t + a:2 * t + a + 1], None, ALU.mult).then_inc(S["on_ready"], 1)
            gained(S["oT_mm"], S["oT_ready"], G_OUT, 0)

            def residual(mm, banks, ready):
                for j in range(4):
                    t, n = divmod(j, 2)
                    dve.wait_ge(mm, j + 1)
                    dve.tensor_tensor(h[:, t, n * 512:(n + 1) * 512], bank[banks[j]][:, :],
                                      h[:, t, n * 512:(n + 1) * 512], ALU.add).then_inc(ready, 1)

            residual(S["wo_mm"], (4, 5, 6, 7), S["h_ready"])
            dve.wait_ge(S["h_sq"], 2)
            mean_square(ss_h, 2, D, S["hlnv"])
            refine(rs_h, 2)
            for t in range(TT):
                dve.tensor_scalar(xn[:, t, :], h[:, t, :], rs_h[:, t:t + 1], None, ALU.mult).then_inc(S["hn_ready"], 1)
            gained(S["hT_mm"], S["hTs_ready"], G_X, 0)
            for u in range(MH * TT):
                dve.wait_ge(S["sm_mm"], u + 1)
                dve.tensor_reduce(nm8[:, u:u + 1], bank[u % 2][:, 0:SEQ], X, ALU.max, negate=True).then_inc(S["pm_ready"], 1)
                dve.wait_ge(S["em_ready"], u + 1)
                link(dve.reciprocal(rd8[:, u:u + 1], dn8[:, u:u + 1]))
                dve.tensor_scalar(prob_m[:, u % NL, :], prob_m[:, u % NL, :], rd8[:, u:u + 1], None,
                                  ALU.mult).then_inc(S["pm_ready"], 1)
            residual(S["wm_mm"], (0, 1, 6, 7), S["h2_ready"])
            dve.wait_ge(S["h2_sq"], 2)
            mean_square(ss_h2, 2, D, S["h2lnv"])
            refine(rs_h2, 2)
            for t in range(TT):
                dve.tensor_scalar(xn[:, t, :], h[:, t, :], rs_h2[:, t:t + 1], None, ALU.mult).then_inc(S["h3_ready"], 1)
            gained(S["h3T_mm"], S["h3T_ready"], G_MOE, 2)
            for t in range(TT):
                dve.wait_ge(S["rt_mm"], t + 1)
                link(dve.tensor_tensor(lg[:, t, :], bank[6 + t][:, 0:NE], brow, ALU.add))
                link(dve.max(top[:, t, :], lg[:, t, :]))
                link(dve.max_index(topi[:, t, :], top[:, t, :], lg[:, t, :]))
                link(dve.tensor_copy(topf[:, t, :], topi[:, t, :]))
                link(dve.tensor_tensor(oh[t], over(cst[:, C_EXP:C_EXP + NE].unsqueeze(1), [P, TOPK, NE]),
                                       over(topf[:, t, 0:TOPK].unsqueeze(2), [P, TOPK, NE]), ALU.is_equal))
                link(dve.tensor_reduce(mask[:, t, :], oh[t].rearrange("p j e -> p e j"), X, ALU.add))
            dve.tensor_copy(mask_bf, mask).then_inc(S["mask_ready"], 1)
            dve.tensor_scalar(nmax0, top[:, :, 0], -1.0, None, ALU.mult).then_inc(S["gate_e"], 1)
            for j in range(2):
                dve.wait_ge(S["split_act"], j + 1)
                dve.tensor_tensor(rest, (rest if j else xn), part[j], ALU.subtract).then_inc(S["split_vec"], 1)
            dve.wait_ge(S["ld_late"], 64)
            link(dve.tensor_copy(bgu[0:96, :], bgu_raw[0:96, :]))
            link(dve.tensor_tensor(bgu_raw[0:96, :], bgu_raw[0:96, :], bgu[0:96, :], ALU.subtract))
            dve.tensor_copy(bgu[32:64, :], bgu_raw[32:64, :])
            link(dve.tensor_copy(bgu[64:96, :], bgu_raw[64:96, :]))
            link(dve.tensor_tensor(bgu_raw[64:96, :], bgu_raw[64:96, :], bgu[64:96, :], ALU.subtract))
            link(dve.tensor_copy(bgu[64:96, :], bgu_raw[64:96, :]))
            dve.wait_ge(S["gate_e"], 3)
            link(dve.reciprocal(ersum, esum))
            for t in range(TT):
                link(dve.tensor_scalar(eg[:, t, :], eg[:, t, :], ersum[:, t:t + 1], None, ALU.mult))
                link(dve.tensor_tensor(oh[t], oh[t], over(eg[:, t, :].unsqueeze(2), [P, TOPK, NE]), ALU.mult))
                dve.tensor_reduce(gates[:, t, 0:NE], oh[t].rearrange("p j e -> p e j"), X, ALU.add).then_inc(S["gates_ready"], 1)
            dve.wait_ge(S["rank_mm"], 1)
            for t in range(TT):
                link(dve.tensor_scalar(place[:, t, 0:NE], mask[:, t, :], BIG, -BIG, ALU.mult, ALU.add))
                link(dve.tensor_tensor(place[:, t, 0:NE], bank[0][:, 32 * t:32 * t + 32], place[:, t, 0:NE], ALU.add))
            link(dve.tensor_copy(cnt, bank[0][:, 64:96]))
            link(dve.tensor_scalar(extra, cnt, float(BLK), None, ALU.is_gt))
            for m in range(2, SEQ // BLK):
                link(dve.scalar_tensor_tensor(extra, cnt, float(m * BLK), extra, ALU.is_gt, ALU.add))
            link(dve.tensor_copy(cum, extra))
            a, b = cum, cum2
            for s in (1, 2, 4, 8, 16):
                dve.tensor_copy(b[:, 0:s], a[:, 0:s])
                link(dve.tensor_tensor(b[:, s:NE], a[:, s:NE], a[:, 0:NE - s], ALU.add))
                a, b = b, a
            total = a
            link(dve.tensor_tensor(beg, total, extra, ALU.subtract))
            item = cst[:, C_ITEM:C_ITEM + NOVF]
            full = [P, NOVF, NE]
            link(dve.tensor_tensor(own, over(item.unsqueeze(2), full), over(beg.unsqueeze(1), full), ALU.is_ge))
            link(dve.tensor_tensor(val, over(item.unsqueeze(2), full), over(total.unsqueeze(1), full), ALU.is_lt))
            link(dve.tensor_tensor(own, own, val, ALU.mult))

            def pick_out(dst, row):
                link(dve.tensor_tensor(val, own, over(row.unsqueeze(1), full), ALU.mult))
                return dve.tensor_reduce(dst, val, X, ALU.add)

            link(pick_out(onehot[:, NE:NITEM], cst[:, C_MOD:C_MOD + NE]))
            link(pick_out(eid_f, cst[:, C_EXP:C_EXP + NE]))
            dve.tensor_copy(onehot[:, 0:NE], cst[:, C_MOD:C_MOD + NE])
            dve.tensor_copy(eid_i, eid_f)
            dve.tensor_copy(novf_i, total[:, NE - 1:NE])
            link(dve.tensor_scalar(beg, beg, float(BLK), -float(BLK), ALU.mult, ALU.add))
            for t in range(TT):
                link(dve.tensor_tensor(cnt, place[:, t, 0:NE], beg, ALU.add))
                link(pick_out(place[:, t, NE:NITEM], cnt))
                link(dve.scalar_tensor_tensor(place[:, t, NE:NITEM], item, -float(BLK), place[:, t, NE:NITEM],
                                              ALU.mult, ALU.add))
                link(pick_out(gates[:, t, NE:NITEM], gates[:, t, 0:NE]))
            dve.memset(o_s, 0.0).then_inc(S["out_copied"], 1)
            dve.memset(gsel, 0.0).then_inc(S["gsel_ready"], 1)
            dve.wait_ge(S["gtT_mm"], 1)
            dve.tensor_copy(gT[0:NE, :], bank[1][0:NE, 0:SEQ]).then_inc(S["gtT_ready"], 1)

            def choose(w):
                for t in range(TT):
                    ins = dve.tensor_scalar(pick[:, t, :], iota[:, 0:BLK], place[:, t, bass.ds(w, 1)], None, ALU.is_equal)
                ins.then_inc(S["pick_ready"], 1)

            def choose_bias(w):
                dve.tensor_copy(bsel[0:96, :], over(onehot[0:96, bass.ds(w, 1)], [96, BLK])).then_inc(S["bsel_ready"], 1)

            def gathered_out(w):
                dve.wait_ge(S["gathered"], w + 1)
                dve.tensor_tensor(spl(xgT, KC), spl(bank[2][:, :], KC),
                                  over(gain[:, G_MOE:G_MOE + KC].unsqueeze(2), [P, KC, BLK]), ALU.mult).then_inc(S["xg_ready"], 1)

            choose(0)
            choose_bias(0)
            dve.tensor_scalar(items_i, total[:, NE - 1:NE], float(NE), None, ALU.add).then_inc(S["counts_ready"], 1)
            gathered_out(0)
            dve.wait_ge(S["counts_ready"], 1)
            items = dve.value_load(items_i[0:1, :], min_val=NE, max_val=NITEM - 1)
            with dve.Fori(0, items) as w:
                nxt = w + 1
                dve.wait_ge(S["gathered"], w + 1)
                choose(nxt)
                dve.wait_ge(S["chunks_used"], w * NCH + 1)
                choose_bias(nxt)
                for t in range(TT):
                    ins = dve.tensor_scalar(gtok[:, t, :], iota, place[:, t, bass.ds(w, 1)],
                                            gates[:, t, bass.ds(w, 1)], ALU.is_equal, ALU.mult)
                ins.then_inc(S["gtok_ready"], 1)
                dve.wait_ge(S["chunks_used"], w * NCH + NGU)
                dve.tensor_scalar(gate_s, bank[0][:, :], LIMIT, None, ALU.min).then_inc(S["gate_ready"], 1)
                dve.tensor_scalar(up_s, bank[1][:, :], LIMIT, -LIMIT, ALU.min, ALU.max).then_inc(S["up_ready"], 1)
                dve.wait_ge(S["gate_ready"], w + 1)
                dve.wait_ge(S["up_ready"], w + 1)
                dve.scalar_tensor_tensor(up_s, up_s, 1.0, gate_s, ALU.add, ALU.mult).then_inc(S["gu_ready"], 1)
                dve.wait_ge(S["sig_ready"], w + 1)
                dve.wait_ge(S["gu_ready"], w + 1)
                dve.tensor_tensor(h_s, up_s, sig_s, ALU.mult).then_inc(S["hmid_ready"], 1)
                gathered_out(nxt)
            dve.wait_ge(S["y_done"], 1)
            for j in range(4):
                t, n = divmod(j, 2)
                dve.tensor_tensor(h[:, t, n * 512:(n + 1) * 512], bank[4 + j][:, :], h[:, t, n * 512:(n + 1) * 512],
                                  ALU.add).then_inc(S["f_ready"], 1)
            dve.wait_ge(S["f_sq"], 2)
            mean_square(ss_f, 2, D, S["flnv"])
            refine(rs_f, 2)
            dve.wait_ge(S["ld_row"], 16)
            for t in range(TT):
                dve.scalar_tensor_tensor(h[:, t, :], h[:, t, :], rs_f[:, t:t + 1], g_row.rearrange("p c n -> p (c n)"), ALU.mult,
                                         ALU.mult).then_inc(S["fin_ready"], 1)

        @block.tensor
        def _(pe):
            mm = pe.matmul

            def transposes(src, ready, done, first_bank, per=1):
                for t in range(TT):
                    pe.wait_ge(ready, per * (t + 1))
                    for b in range(2):
                        for j in range(4):
                            c = 4 * b + j
                            ins = pe.transpose(bank[first_bank + 2 * t + b][:, j * P:(j + 1) * P],
                                               src[:, t, c * P:(c + 1) * P], ident)
                        ins.then_inc(done, 1)

            pe.wait_ge(S["ld_cst"], 32)
            transposes(xn, S["xn_ready"], S["xT_mm"], 0)
            pe.wait_ge(S["xT_ready"], 4)
            for k in range(KC):
                pe.wait_ge(ld_win[k], 16)
                for t in range(TT):
                    for n in range(4):
                        ins = mm(bank[4 * t + n][:, 0:ZN], nT[:, k, t * P:(t + 1) * P], win[:, k, n * ZN:(n + 1) * ZN],
                                 start=(k == 0), stop=(k == KC - 1))
                        if k == KC - 1:
                            ins.then_inc(S["z_mm"], 1)
            pe.wait_ge(S["z_act"], 2)
            pe.wait_ge(S["z_vec"], 2)
            transposes(v_mem, S["memn_ready"], S["mT_mm"], 0)
            pe.wait_ge(S["z_act"], 4)
            pe.wait_ge(S["z_vec"], 4)
            pe.wait_ge(S["mT_ready"], 4)
            for c in range(KC):
                for k in range(KC):
                    if c == 0:
                        pe.wait_ge(ld_wmkv[k], 16)
                    ins = mm(bank[4 + c // 2][:, c % 2 * SEQ:(c % 2 + 1) * SEQ], wmkv[:, k, c * P:(c + 1) * P], nT[:, k, :],
                             start=(k == 0), stop=(k == KC - 1))
                if c % 2:
                    ins.then_inc(S["kT_mm"], 1)
            for t in range(TT):
                for n in range(2):
                    for k in range(KC):
                        ins = mm(bank[2 * t + n][:, :], nT[:, k, t * P:(t + 1) * P], wmkv[:, k, D + n * 512:D + (n + 1) * 512],
                                 start=(k == 0), stop=(k == KC - 1))
                    ins.then_inc(S["v_mm"], 1)
            pe.wait_ge(S["zn_ready"], 4)
            pe.wait_ge(S["kT_ready"], 4)
            for c in range(3):
                for t in range(TT):
                    ins = pe.transpose(bank[4 + c // 2][:, c % 2 * SEQ + t * P:c % 2 * SEQ + (t + 1) * P],
                                       zn[:, t, c * P:(c + 1) * P], ident)
            ins.then_inc(S["zT_mm"], 1)
            pe.wait_ge(S["zT_ready"], 2)
            pe.wait_ge(S["ld_lora"], 32)
            pe.wait_ge(S["v_ready"], 4)
            for t in range(TT):
                for n in range(2):
                    for k in range(2):
                        ins = mm(bank[2 * t + n][:, 0:384], znT[:, k, t * P:(t + 1) * P], wqb[:, k, n * 384:(n + 1) * 384],
                                 start=(k == 0), stop=(k == 1))
                    ins.then_inc(S["qb_mm"], 1)
            for t in range(TT):
                for n in range(2):
                    mm(bank[4 + 2 * t + n][:, :], znT[:, 2, t * P:(t + 1) * P], wkvb[:, n * 512:(n + 1) * 512],
                       start=True, stop=True).then_inc(S["kvb_mm"], 1)

            def bias_fill(f):
                hf, t, g, s = f // 16, f // 8 % 2, f // 2 % 4, f % 2
                pe.wait_ge(S["bias_ev"], f - 3) if f >= 4 else pe.wait_ge(S["qb_ready"], 4)
                for k in range(16):
                    ins = mm(bank[f % 4][:, 24 * k:24 * k + 24], steps[32 * g:32 * g + 32, s * 16 + k, t * P:(t + 1) * P],
                             delta[32 * g:32 * g + 32, :, :], start=True, stop=True)
                ins.then_inc(S["bias_mm"], 1)

            pe.wait_ge(S["kvb_ready"], 4)
            for c in range(8):
                for t in range(TT):
                    ins = pe.transpose(bank[4 + c // 2][:, c % 2 * SEQ + t * P:c % 2 * SEQ + (t + 1) * P],
                                       z[:, t, c * P:(c + 1) * P], ident)
                if c % 2:
                    ins.then_inc(S["aT_mm"], 1)
            pe.wait_ge(S["steps_ready"], 1)
            for f in range(16):
                bias_fill(f)
            pe.wait_ge(S["qTa_ready"], 2)
            pe.wait_ge(S["kTa_ready"], 2)
            pe.wait_ge(S["ropek_ready"], 2)
            for src, ready, done in ((qb, None, S["q96_mm"]), (k96, S["q96_ready"], S["k96_mm"])):
                for j in range(4):
                    if ready is not None:
                        pe.wait_ge(ready, j + 1)
                    for hd in (2 * j, 2 * j + 1):
                        for t in range(TT):
                            ins = pe.transpose(bank[4 + j][0:DQB, hd % 2 * SEQ + t * P:hd % 2 * SEQ + (t + 1) * P],
                                               src[:, t, hd * DQB:(hd + 1) * DQB], ident)
                    ins.then_inc(done, 1)
            pe.wait_ge(S["steps_ready"], 2)
            for f in range(16, 32):
                bias_fill(f)

            def scores(u):
                a, hd, t = u // 16, u % 16 // TT, u % TT
                if u >= 2:
                    pe.wait_ge(S["s_read"], u - 1)
                    if u - 2 >= NU // 2:
                        pe.wait_ge(S["e_ready"], u - 1)
                if a == 0:
                    lo = hd % 2 * DH
                    q, k = qT_a[lo:lo + DH, hd // 2, t * P:(t + 1) * P], kT_a[lo:lo + DH, hd // 2, :]
                else:
                    q, k = qT96[0:DQB, hd, t * P:(t + 1) * P], kT96[0:DQB, hd, :]
                mm(bank[u % 2][:, 0:SEQ], q, k, start=True, stop=True).then_inc(S["s_mm"], 1)

            def probs_transposed(u):
                pe.wait_ge(S["e_ready"], u + 1)
                if u >= 2:
                    pe.wait_ge(S["pT_ready"], u - 1)
                for m in range(TT):
                    ins = pe.transpose(bank[(2, 7)[u % 2]][:, m * P:(m + 1) * P], prob[:, u % NL, m * P:(m + 1) * P], ident)
                ins.then_inc(S["pT_mm"], 1)

            def outputs(u):
                a, hd, t = u // 16, u % 16 // TT, u % TT
                pe.wait_ge(S["pT_ready"], u + 1)
                for m in range(TT):
                    v = z[:, m, 2 * WA + hd * DH:2 * WA + (hd + 1) * DH] if a == 0 else v_b[:, m, hd * DH:(hd + 1) * DH]
                    ins = mm(bank[3 + 2 * a + t][:, hd * DH:(hd + 1) * DH], probT[:, u % NL, m * P:(m + 1) * P], v,
                             start=(m == 0), stop=(m == TT - 1))
                ins.then_inc(S["pv_mm"], 1)

            pe.wait_ge(S["bias_ev"], 32)
            pe.wait_ge(S["k96_ready"], 4)
            for i in range(NU + 3):
                if i < NU:
                    scores(i)
                if 0 <= i - 2 < NU:
                    probs_transposed(i - 2)
                if 0 <= i - 3 < NU:
                    outputs(i - 3)
            transposes(o_cat, S["on_ready"], S["oT_mm"], 0, per=2)

            def square(done, banks):
                for t in range(TT):
                    for n in range(2):
                        for k in range(KC):
                            ins = mm(bank[banks[2 * t + n]][:, :], src_T[:, k, t * P:(t + 1) * P],
                                     w_sq[:, k, n * 512:(n + 1) * 512], start=(k == 0), stop=(k == KC - 1))
                        ins.then_inc(done, 1)

            pe.wait_ge(S["oT_ready"], 4)
            pe.wait_ge(S["ld_wo"], 16)
            src_T = nT
            square(S["wo_mm"], (4, 5, 6, 7))
            transposes(xn, S["hn_ready"], S["hT_mm"], 0)
            pe.wait_ge(S["hTs_ready"], 4)
            pe.wait_ge(S["h_ready"], 4)
            for c in range(KC):
                for k in range(KC):
                    if c == 0 and k % 2 == 0:
                        pe.wait_ge(ld_wmq[k // 2], 16)
                    ins = mm(bank[4 + c // 2][:, c % 2 * SEQ:(c % 2 + 1) * SEQ], wmq[:, k, c * P:(c + 1) * P], nT[:, k, :],
                             start=(k == 0), stop=(k == KC - 1))
                if c % 2:
                    ins.then_inc(S["qm_mm"], 1)
            pe.wait_ge(S["qm_ready"], 4)

            def mem_scores(u):
                hd, t = divmod(u, TT)
                if u >= 2:
                    pe.wait_ge(S["em_ready"], u - 1)
                for j in range(2):
                    c = 2 * hd + j
                    ins = mm(bank[u % 2][:, 0:SEQ], qT_m[:, c, t * P:(t + 1) * P], kT_mem[:, c, :], start=(j == 0), stop=(j == 1))
                ins.then_inc(S["sm_mm"], 1)

            def mem_outputs(hd):
                pe.wait_ge(S["pm_ready"], 4 * hd + 4)
                if hd >= 2:
                    pe.wait_ge(S["pmT_ready"], hd - 1)
                for t in range(TT):
                    for m in range(TT):
                        ins = pe.transpose(bank[2 + hd % 2][:, m * SEQ + t * P:m * SEQ + (t + 1) * P],
                                           prob_m[:, (2 * hd + t) % NL, m * P:(m + 1) * P], ident)
                ins.then_inc(S["pmT_mm"], 1)

            def mem_values(hd):
                pe.wait_ge(S["pmT_ready"], hd + 1)
                if hd >= 2:
                    pe.wait_ge(S["om_ready"], hd - 1)
                for j in range(2):
                    for m in range(TT):
                        c = 2 * hd + j
                        ins = mm(bank[4 + hd % 2][:, j * SEQ:(j + 1) * SEQ], v_mem[:, m, c * P:(c + 1) * P],
                                 probT_m[:, hd % 2, m, :], start=(m == 0), stop=(m == TT - 1))
                ins.then_inc(S["om_mm"], 1)

            mem_scores(0)
            mem_scores(1)
            for hd in range(MH):
                if hd + 1 < MH:
                    mem_scores(2 * hd + 2)
                    mem_scores(2 * hd + 3)
                mem_outputs(hd)
                if hd >= 1:
                    mem_values(hd - 1)
            mem_values(MH - 1)
            pe.wait_ge(S["om_ready"], MH)
            pe.wait_ge(S["ld_wmo"], 16)
            src_T = oT_m
            square(S["wm_mm"], (0, 1, 6, 7))
            transposes(xn, S["h3_ready"], S["h3T_mm"], 2)
            pe.wait_ge(S["h3T_ready"], 4)
            pe.wait_ge(S["h2_ready"], 4)
            pe.wait_ge(S["ld_wr"], 16)
            for t in range(TT):
                for k in range(KC):
                    ins = mm(bank[6 + t][:, 0:NE], nT[:, k, t * P:(t + 1) * P], wr[:, k, :], start=(k == 0), stop=(k == KC - 1))
                ins.then_inc(S["rt_mm"], 1)
            pe.wait_ge(S["mask_ready"], 1)
            pe.wait_ge(S["ones_ready"], 1)
            mm(bank[0][:, 0:32], up_bf[:, :], mask_bf[:, 0, :], start=True, stop=True)
            mm(bank[0][:, 32:64], ones_bf[:, :], mask_bf[:, 0, :], start=True, stop=False)
            mm(bank[0][:, 32:64], up_bf[:, :], mask_bf[:, 1, :], start=False, stop=True)
            mm(bank[0][:, 64:96], ones_bf[:, :], mask_bf[:, 0, :], start=True, stop=False)
            mm(bank[0][:, 64:96], ones_bf[:, :], mask_bf[:, 1, :], start=False, stop=True).then_inc(S["rank_mm"], 1)
            pe.wait_ge(S["gates_ready"], 2)
            for t in range(TT):
                ins = pe.transpose(bank[1][0:NE, t * P:(t + 1) * P], gates[:, t, 0:NE], ident)
            ins.then_inc(S["gtT_mm"], 1)
            pe.wait_ge(S["gtT_ready"], 1)
            pe.wait_ge(S["ld_late"], 64)
            for t in range(TT):
                for n in range(2):
                    ins = mm(bank[4 + 2 * t + n][:, :], gT[0:NE, t * P:(t + 1) * P], bdn[0:NE, n * 512:(n + 1) * 512],
                             start=True, stop=False, skip_group_check=True)
            ins.then_inc(S["y_init"], 1)

            def gather():
                for c in range(KC):
                    for j in range(3):
                        for t in range(TT):
                            ins = mm(bank[2][:, c * BLK:(c + 1) * BLK], part[j][:, t, c * P:(c + 1) * P], pick[:, t, :],
                                     start=(j == 0 and t == 0), stop=(j == 2 and t == TT - 1))
                ins.then_inc(S["gathered"], 1)

            def scatter(last=False):
                for t in range(TT):
                    for n in range(2):
                        lo = n * BLK
                        ins = mm(bank[4 + 2 * t + n][:, :], gsel[lo:lo + BLK, t * P:(t + 1) * P], o_s[lo:lo + BLK, :],
                                 start=False, stop=last, skip_group_check=True)
                return ins

            pe.wait_ge(S["split_act"], 3)
            pe.wait_ge(S["pick_ready"], 1)
            gather()
            pe.wait_ge(S["counts_ready"], 1)
            items = pe.value_load(items_i[0:1, :], min_val=NE, max_val=NITEM - 1)
            with pe.Fori(0, items) as w:
                nxt = w + 1
                pe.wait_ge(S["xg_ready"], nxt)
                pe.wait_ge(S["bsel_ready"], nxt)
                for n in range(4):
                    lo = n % 2 * BLK
                    mm(bank[n // 2][lo:lo + BLK, :], bsel[0:96, :], bgu[0:96, n * 512:(n + 1) * 512], start=True, stop=False)
                for k in range(NGU):
                    pe.wait_ge(ld_exp[k], w * 16 + 16)
                    for n in range(4):
                        lo = n % 2 * BLK
                        ins = mm(bank[n // 2][lo:lo + BLK, :], xgT[:, k * BLK:(k + 1) * BLK],
                                 slot(k)[:, n * 512:(n + 1) * 512], start=False, stop=(k == NGU - 1))
                    ins.then_inc(S["chunks_used"], 1)
                pe.wait_ge(S["gsel_ready"], nxt)
                pe.wait_ge(S["pick_ready"], w + 2)
                gather()
                pe.wait_ge(S["out_copied"], nxt)
                scatter().then_inc(S["scattered"], 1)
                pe.wait_ge(S["xg_ready"], w + 2)
                pe.wait_ge(S["hmid_ready"], nxt)
                for j in range(4):
                    ins = pe.transpose(bank[2][:, j * P:(j + 1) * P], h_s[:, j * P:(j + 1) * P], ident)
                ins.then_inc(S["hid_mm"], 1)
                pe.wait_ge(S["hid_ready"], nxt)
                for c in range(NDN):
                    pe.wait_ge(ld_exp[NGU + c], w * 16 + 16)
                    for j in range(2):
                        f = 2 * c + j
                        lhs = hT[:, f % 4 * P + f // 4 * BLK:f % 4 * P + f // 4 * BLK + BLK]
                        for n in range(2):
                            ins = mm(bank[3][n * BLK:(n + 1) * BLK, :], lhs,
                                     slot(NGU + c)[:, j * D + n * 512:j * D + (n + 1) * 512],
                                     start=(f == 0), stop=(f == 7))
                    ins.then_inc(S["chunks_used"], 1)
                pe.wait_ge(S["gtok_ready"], nxt)
                for t in range(TT):
                    ins = pe.transpose(bank[2][:, t * P:(t + 1) * P], gtok[:, t, :], ident)
                ins.then_inc(S["gsel_mm"], 1)
            pe.wait_ge(S["out_copied"], items + 1)
            pe.wait_ge(S["gsel_ready"], items + 1)
            scatter(last=True).then_inc(S["y_done"], 1)


def kernel(x, mem, positions, g_mix, w_in, g_q_a, w_q_b, g_kv_a, w_kv_b, rel_bias, g_out_a, g_out_b, w_o,
           g_xattn, g_mem, w_mq, w_mkv, w_mo, g_moe, w_router, b_router, w_gate_up, b_gate_up, w_down,
           b_down, g_final):
    import concourse.bacc as bacc
    from concourse.bass_utils import run_bass_kernel_spmd

    def cols(g):
        return np.asarray(g).reshape(-1, P).T

    pos = np.ascontiguousarray(np.asarray(positions)[0])
    rel = np.asarray(rel_bias)
    rel_cur = np.concatenate([rel[ORDER], rel[:1]])
    rel_prev = np.concatenate([np.zeros((1, HEADS), rel.dtype), rel[ORDER]])
    ins = {
        "x": np.asarray(x)[0], "mem": np.asarray(mem)[0], "pos": pos, "pos_col": pos.reshape(TT, P).T,
        "posk": np.repeat(pos.reshape(4, SEQ // 4), NB, axis=0),
        "consts": shape_constants(),
        "gains": np.concatenate([cols(g_mix), cols(g_xattn), cols(g_mem), cols(g_moe), cols(g_out_a),
                                 cols(g_out_b), cols(g_q_a), cols(g_kv_a)], axis=1),
        "w_in": w_in[0], "w_q_b": w_q_b[0], "w_kv_b": w_kv_b[0],
        "rel_cur": np.tile(rel_cur, (P // NB, 1)), "rel_prev": np.tile(rel_prev, (P // NB, 1)),
        "w_o": w_o[0], "w_mq": w_mq[0], "w_mkv": w_mkv[0], "w_mo": w_mo[0],
        "w_router": w_router[0], "b_router": b_router[0], "w_gate_up": w_gate_up[0],
        "b_gate_up": b_gate_up[0], "w_down": w_down[0], "b_down": b_down[0], "g_final": g_final,
    }
    nc = bacc.Bacc("TRN2", target_bir_lowering=False, num_devices=1)
    arrays, args = {}, []
    for name, a in ins.items():
        a = np.ascontiguousarray(a)
        arrays[f"in_{name}"] = a
        args.append(nc.dram_tensor(f"in_{name}", a.shape, mybir.dt.from_np(a.dtype), kind="ExternalInput").ap())
    args.append(nc.dram_tensor("out", (SEQ, D), mybir.dt.float32, kind="ExternalOutput").ap())
    encoder_kernel(nc, *args)
    r = run_bass_kernel_spmd(nc, [arrays], core_ids=[0])
    return r.results[0]["out"].reshape(1, SEQ, D)
```

```python
import concourse.bass as bass
from concourse import mybir
from contextlib import ExitStack
import numpy as np

P = 128
D = 1024
SEQ = 256
TT = SEQ // P
KC = D // P
HEADS, DH = 8, 64
WA = HEADS * DH
QL, KVL = 256, 128
ROPE, NOPE = 32, 64
DQB = NOPE + ROPE
ZW = 3 * WA + QL + KVL + ROPE
ZN = ZW // 4
MH, MDH = 4, 256
NB = 32
NE, TOPK = 32, 4
BLK = 64
NOVF = SEQ * TOPK // BLK
NITEM = NE + NOVF
SLOT = 2048
NGU, NDN = 8, 4
NCH = NGU + NDN
EPS = 1e-6
NORMS = ("x", "mem", "z", "o", "h", "h2", "f")
BIG = 4096.0
LIMIT, ALPHA = 7.0, 1.702
PATTERNS = ((128, 1), (512, 4), (2048, 16))
LARGE = (8, 15, 27, 50, 91, 166, 305, 559)
FROM = list(range(8)) + list(LARGE)
ORDER = list(range(15, 0, -1)) + [0] + list(range(17, 32))
STEPS = [-1e9] + [1 - FROM[b + 1] for b in range(14, 0, -1)] + [0] + [FROM[b - 16] for b in range(17, 32)]

C_ID = 0
C_LOGM = C_ID + P
C_UP = C_LOGM + TT * SEQ
C_IOTA = C_UP + P
C_EXP = C_IOTA + P
C_STEP = C_EXP + NE
C_FREQ = C_STEP + 1
C_MOD = C_FREQ + ROPE // 2
C_ITEM = C_MOD + NE
C_PMOD = C_ITEM + NITEM
C_END = C_PMOD + 1
G_MIX, G_X, G_MEM, G_MOE, G_OUT, G_QA, G_KVA = 0, 8, 16, 24, 32, 40, 42
G_END = 43


def shape_constants():
    c = np.zeros((P, C_END), np.float32)
    p = np.arange(P)
    c[:, C_ID:C_ID + P] = np.eye(P)
    for t in range(TT):
        off = np.arange(SEQ)[None, :] - (t * P + p)[:, None]
        n = sum(((off % d == 0) & (np.abs(off) <= w // 2)).astype(int) for w, d in PATTERNS)
        c[:, C_LOGM + t * SEQ:C_LOGM + (t + 1) * SEQ] = np.where(n > 0, np.log(np.maximum(n, 1)), -1e30)
    c[:, C_UP:C_UP + P] = p[:, None] < p[None, :]
    c[:, C_IOTA:C_IOTA + P] = p[None, :] % BLK
    c[:, C_EXP:C_EXP + NE] = np.arange(NE)[None, :]
    c[:, C_STEP] = (STEPS + [1e9])[0:NB] * (P // NB)
    c[:, C_FREQ:C_FREQ + ROPE // 2] = np.float32(10000.0) ** (-np.arange(0, ROPE, 2, dtype=np.float32) / ROPE)
    c[:, C_MOD:C_MOD + NE] = (p % NE)[:, None] == np.arange(NE)[None, :]
    c[:, C_ITEM:C_ITEM + NITEM] = np.arange(NITEM)[None, :]
    c[:, C_PMOD] = p % NE
    return c


def encoder_kernel(nc, x, mem, pos, pos_col, posk, consts, gains, w_in, w_q_b, w_kv_b, rel_cur, rel_prev, w_o,
                   w_mq, w_mkv, w_mo, w_router, b_router, w_gate_up, b_gate_up, w_down, b_down,
                   g_final, out):
    f32, bf16 = mybir.dt.float32, mybir.dt.bfloat16
    i32, u32 = mybir.dt.int32, mybir.dt.uint32
    ALU = mybir.AluOpType
    ACT = mybir.ActivationFunctionType
    X = mybir.AxisListType.X

    ctx = ExitStack()
    with ctx:
        def sb(name, cols, dt=f32):
            return ctx.enter_context(nc.sbuf_tensor(name, [P, cols], dt))

        ring = sb("ring", NCH * SLOT)
        stage = sb("stage", KC * ZW)
        h = sb("h", TT * D)[:, :].rearrange("p (t d) -> p t d", t=TT)
        kT_mem = sb("kT_mem", KC * SEQ)[:, :].rearrange("p (c m) -> p c m", c=KC)
        v_mem = sb("v_mem", TT * D)[:, :].rearrange("p (t d) -> p t d", t=TT)
        nT_flat = sb("nT", KC * SEQ)
        nT = nT_flat[:, :].rearrange("p (c m) -> p c m", c=KC)
        spare = sb("spare", TT * D)
        cst = sb("cst", C_END)
        gain = sb("gain", G_END)
        ones_bf = sb("ones_bf", P, bf16)
        up_bf = sb("up_bf", P, bf16)
        stat = sb("stat", 218)
        one = sb("one", 1)
        trig = sb("trig", 6 * 32)

        def in_ring(lo, n):
            return ring[:, lo:lo + n]

        def in_stage(lo, n):
            return stage[:, lo:lo + n]

        def spl(ap, t):
            return ap.rearrange("p (t d) -> p t d", t=t)

        def slot(c):
            return ring[:, c * SLOT:(c + 1) * SLOT]

        def over(ap, shape):
            return ap.to_broadcast(shape)

        ident = cst[:, C_ID:C_ID + P]
        iota = cst[:, C_IOTA:C_IOTA + P]
        win = spl(in_stage(0, KC * ZW), KC)
        wmkv = spl(in_ring(0, KC * 2 * D), KC)
        z = spl(in_stage(0, TT * ZW), TT)
        bias = in_stage(3904, TT * HEADS * SEQ).rearrange("p (t h k) -> p t h k", t=TT, h=HEADS)
        qb = spl(in_stage(8000, TT * HEADS * DQB), TT)
        k96 = spl(in_stage(9536, TT * HEADS * DQB), TT)
        v_b = spl(in_stage(11072, TT * WA), TT)
        NL = 4
        logit = spl(in_stage(12096, NL * SEQ), NL)
        prob = spl(in_stage(13120, NL * SEQ), NL)
        probT = in_stage(14144, 2 * TT * SEQ).rearrange("p (j m q) -> p j m q", j=2, m=TT)
        tail = 2 * KC * D
        steps = in_ring(tail, 4096).bitcast(bf16).rearrange("p (k q) -> p k q", q=SEQ)
        qT96 = spl(in_ring(tail, HEADS * SEQ), HEADS)
        kT96 = spl(in_ring(tail + 2048, HEADS * SEQ), HEADS)
        wqb = spl(in_ring(tail + 4096, 2 * HEADS * DQB), 2)
        wkvb = in_ring(tail + 5632, HEADS * (NOPE + DH))
        znT = spl(in_ring(tail + 6656, 3 * SEQ), 3)
        rope_t = in_ring(tail + 7424, 4 * HEADS * ROPE // 2)
        square_s = spl(in_ring(tail + 6656, 2 * SEQ), 2)
        qT_a = spl(spare[:, 0:4 * SEQ], 4)
        kT_a = spl(spare[:, 4 * SEQ:8 * SEQ], 4)
        oT = nT
        wo = spl(in_ring(0, KC * D), KC)
        wmq = spl(in_ring(KC * D, KC * D), KC)
        wmo = spl(in_stage(0, KC * D), KC)
        hT_s = spl(spare[:, :], KC)
        qT_m = spl(in_stage(8192, KC * SEQ), KC)
        prob_m = spl(in_stage(10240, NL * SEQ), NL)
        probT_m = in_stage(11264, 2 * TT * SEQ).rearrange("p (j m q) -> p j m q", j=2, m=TT)
        wr = spl(in_stage(12288, KC * NE), KC)
        bdn = in_stage(12544, D)
        bgu_raw = in_stage(13568, 2 * D)
        oT_m = nT
        part = [ap.bitcast(bf16).rearrange("p (t d) -> p t d", t=TT)
                for ap in (in_stage(0, D), in_stage(D, D), in_stage(2 * D, D))]
        rest = v_mem
        xgT = in_stage(5120, 512)
        gate_s, up_s, sig_s, h_s = (in_stage(5632 + 512 * i, 512) for i in range(4))
        hT = in_stage(7680, 512)
        o_s = in_stage(8192, 512)
        gsel = in_stage(8704, TT * P)
        gtok = spl(in_stage(8960, TT * P), TT)
        bgu = in_stage(9216, D).bitcast(bf16)
        pick = spl(in_stage(3072, TT * BLK // 2).bitcast(bf16), TT)
        bsel = in_stage(3136, BLK // 2).bitcast(bf16)
        rt = in_stage(3200, 1664)
        gT = in_stage(4864, SEQ)
        own, val = (spl(a[:, 0:NITEM * NE], NITEM) for a in (nT_flat, spare))
        g_row = kT_mem[:, 0:4, :]

        bank = [ctx.enter_context(nc.psum_tensor(f"bank{i}", [P, 512], f32)) for i in range(8)]

        names = """
            ends_ready first_ready tables_ready x_done ms_ready root_ready
            ld_x ld_id ld_mem ld_cst ld_small ld_lora ld_wo ld_wmq ld_wmo ld_wr ld_late ld_row st_out
            vec_chain
            x_sq xT_mm xT_ready z_mm z_act z_vec mem_sq memn_ready mT_mm mT_ready
            trig_in sin_ready ones_ready zT_mm zT_ready z_sq zroot_ready qb_mm qb_ready kvb_mm
            kvb_ready kT_mm kT_ready v_mm v_ready aT_mm qTa_ready kTa_ready steps_ready bias_mm bias_ev
            ropek_ready q96_mm q96_ready k96_mm k96_ready s_mm s_read e_ready p_ready pT_mm pT_ready pv_mm
            oT_ready osq_ready oss_mm oss_ready ocol_mm ocol_read wo_mm h_ready h_sq
            hroot_ready hT_mm hTs_ready qm_mm qm_ready sm_mm mmax_ready em_ready pm_ready pmT_mm pmT_ready
            om_mm om_ready wm_mm h2_ready h2_sq h3T_mm h3T_ready rt_mm rt_read xs_ready
            split_act split_pool split_vec mask_ready rank_mm gate_in gate_e gates_ready gtT_mm gtT_ready counts_ready
            chunks_used gathered xg_ready scattered hid_mm hid_ready out_copied gsel_mm gsel_ready
            pick_ready bsel_ready gtok_ready gate_ready sig_ready up_ready gu_ready hmid_ready
            y_done f_ready f_sq fin_ready
        """.split()
        S = {n: ctx.enter_context(nc.semaphore(n)) for n in names}
        ld_win = [ctx.enter_context(nc.semaphore(f"ld_win{k}")) for k in range(KC)]
        ld_ring = [ctx.enter_context(nc.semaphore(f"ld_ring{c}")) for c in range(NCH)]

        def rt2(lo, n):
            return rt[:, lo:lo + TT * n].rearrange("p (t n) -> p t n", t=TT)
        lg = rt2(0, NE)
        top = rt2(64, 8)
        topi = rt[:, 80:96].bitcast(u32).rearrange("p (t n) -> p t n", t=TT)
        topf = rt2(96, 8)
        eg = rt2(112, TOPK)
        oh = [rt[:, 128 + i * TOPK * NE:128 + (i + 1) * TOPK * NE].rearrange("p (j e) -> p j e", j=TOPK)
              for i in range(TT)]
        mask = rt2(384, NE)
        mask_bf = rt[:, 448:448 + NE].bitcast(bf16).rearrange("p (t n) -> p t n", t=TT)
        place = rt2(480, NITEM)
        gates = rt2(576, NITEM)
        onehot = rt[:, 672:672 + NITEM]
        cnt, extra, cum, cum2, beg = (rt[:, 720 + 32 * i:720 + 32 * (i + 1)] for i in range(5))
        total_f = rt[:, 940:941]
        items_i = rt[:, 944:945].bitcast(i32)
        place_e = rt2(992, NE)
        gates_e = rt2(1056, NE)
        eid_f = rt[:, 1120:1120 + NITEM]
        eid_i = rt[:, 1168:1168 + NITEM].bitcast(i32)
        last_i = rt[:, 1248:1248 + NE].bitcast(i32)
        nmax0, esum, ersum = rt[:, 980:982], rt[:, 984:986], rt[:, 988:990]

        def st(lo, n):
            return stat[:, lo:lo + n]
        stats_of = {n: (st(16 * i, 4), st(16 * i + 4, 4), st(16 * i + 8, 4), st(16 * i + 12, 4))
                    for i, n in enumerate(NORMS)}
        nwt = st(112, 4)
        NU = 2 * HEADS * TT
        nmax, den, rden = st(116, NU), st(148, NU), st(180, NU)
        brow = trig[:, 160:192]
        poscol, posrow = sb("poscol", TT), sb("posrow", SEQ)
        poscol_i, posrow_i = sb("poscol_i", TT, i32), sb("posrow_i", SEQ, i32)
        posk_i, posk_f = sb("posk_i", SEQ // 4, i32), sb("posk_f", SEQ // 4)
        relc, relp = sb("relc", HEADS), sb("relp", HEADS)
        delta = sb("delta", HEADS * 3, bf16)[:, :].rearrange("p (h s) -> p h s", s=3)
        nm8, dn8, rd8 = sb("nm8", 8), sb("dn8", 8), sb("rd8", 8)
        oss_row = spare[:, 0:2 * SEQ]
        mark = sb("mark", 4)
        WO_BANKS = (0, 1, 2, 3, 6, 4, 5, 7)
        square_early, square_late = in_stage(8192, TT * D), in_stage(10240, TT * D)

        block = ctx.enter_context(nc.Block())

        @block.sync
        def _(sp):
            sp.dma_start(ident, consts[:, C_ID:C_ID + P]).then_inc(S["ld_id"], 16)
            for t in range(TT):
                sp.dma_start(h[:, t, :], x[t * P:(t + 1) * P, :]).then_inc(S["ld_x"], 16)
            sp.dma_start(gain[:, :], gains).then_inc(S["ld_cst"], 16)
            sp.dma_start(win[:, 0, :], w_in[0:P, :]).then_inc(ld_win[0], 16)
            sp.dma_start(cst[:, C_LOGM:C_END], consts[:, C_LOGM:C_END]).then_inc(S["ld_cst"], 16)
            for k in range(1, KC):
                sp.dma_start(win[:, k, :], w_in[k * P:(k + 1) * P, :]).then_inc(ld_win[k], 16)
                if k == 3:
                    sp.dma_start(v_mem, mem.rearrange("(t p) d -> p t d", p=P)).then_inc(S["ld_mem"], 16)
            for k in range(KC):
                sp.dma_start(wmkv[:, k, :], w_mkv[k * P:(k + 1) * P, :]).then_inc(ld_ring[k], 16)
                if k == 1:
                    sp.dma_start(wqb, w_q_b.rearrange("(c p) n -> p c n", p=P)).then_inc(S["ld_lora"], 16)
                    sp.dma_start(wkvb, w_kv_b).then_inc(S["ld_lora"], 16)
            sp.wait_ge(S["v_mm"], 4)
            sp.dma_start(wo, w_o.rearrange("(c p) n -> p c n", p=P)).then_inc(S["ld_wo"], 16)
            sp.dma_start(wmq, w_mq.rearrange("(c p) n -> p c n", p=P)).then_inc(S["ld_wmq"], 16)
            sp.wait_ge(S["pv_mm"], HEADS * 2)
            sp.dma_start(wmo, w_mo.rearrange("(c p) n -> p c n", p=P)).then_inc(S["ld_wmo"], 16)
            sp.dma_start(wr, w_router.rearrange("(c p) n -> p c n", p=P)).then_inc(S["ld_wr"], 16)
            sp.dma_start(bdn[0:NE, :], b_down).then_inc(S["ld_late"], 16)
            for j in range(3):
                sp.dma_start(bgu_raw[NE * j:NE * (j + 1), :], b_gate_up).then_inc(S["ld_late"], 16)

            def load_chunk(c, e):
                if c < NGU:
                    sp.dma_start(slot(c), w_gate_up[e, c * P:(c + 1) * P, :]).then_inc(ld_ring[c], 16)
                else:
                    f = 2 * (c - NGU) * P
                    sp.dma_start(spl(slot(c), 2), w_down[e, f:f + 2 * P, :].rearrange("(j p) n -> p j n", p=P))\
                        .then_inc(ld_ring[c], 16)

            sp.wait_ge(S["oss_mm"], 8)
            for c in range(NGU, NCH):
                load_chunk(c, 0)
            sp.wait_ge(S["wo_mm"], 8)
            for c in range(0, 4):
                load_chunk(c, 0)
            sp.wait_ge(S["qm_mm"], 4)
            for c in range(4, NGU):
                load_chunk(c, 0)
            sp.wait_ge(S["sm_mm"], MH * TT)
            sp.dma_start(g_row, g_final.rearrange("(a c n) -> a c n", a=1, c=4).to_broadcast([P, 4, SEQ])).then_inc(S["ld_row"], 16)
            wgu = w_gate_up.rearrange("e (c p) n -> c p e n", p=P)
            wdn = w_down.rearrange("e (c j p) n -> c p e j n", j=2, p=P)

            def load_next(c, e, used):
                sp.wait_ge(S["chunks_used"], used)
                if c < NGU:
                    sp.dma_start(slot(c), wgu[c, :, bass.ds(e, 1), :]).then_inc(ld_ring[c], 16)
                else:
                    sp.dma_start(spl(slot(c), 2), wdn[c - NGU, :, bass.ds(e, 1), :, :]).then_inc(ld_ring[c], 16)

            sp.wait_ge(S["ends_ready"], 1)
            with sp.Fori(1, NE) as e:
                last = sp.value_load(last_i[0:1, bass.ds(e - 1, 1)], min_val=0, max_val=NITEM - 1)
                for c in range(NCH):
                    load_next(c, e, last * NCH + (c + 1))
            for t in range(TT):
                sp.wait_ge(S["fin_ready"], t + 1)
                sp.dma_start(out[t * P:(t + 1) * P, :], h[:, t, :]).then_inc(S["st_out"], 16)
            sp.wait_ge(S["st_out"], 16 * TT)

        @block.scalar
        def _(act):
            act.dma_start(poscol_i[:, :], pos_col).then_inc(S["ld_small"], 16)
            act.dma_start(posrow_i[:, :], pos.rearrange("(a n) -> a n", a=1).to_broadcast([P, SEQ])).then_inc(S["ld_small"], 16)
            act.dma_start(posk_i[:, :], posk).then_inc(S["ld_small"], 16)
            act.dma_start(relc[:, :], rel_cur).then_inc(S["ld_small"], 16)
            act.dma_start(relp[:, :], rel_prev).then_inc(S["ld_small"], 16)
            act.dma_start(brow, b_router.rearrange("(a n) -> a n", a=1).to_broadcast([P, NE])).then_inc(S["ld_small"], 16)

            def root(of, n):
                ms, y0 = stats_of[of][1][:, 0:n], stats_of[of][2][:, 0:n]
                act.wait_ge(S["ms_ready"], NORMS.index(of) + 1)
                act.activation(y0, ms, ACT.Sqrt).then_inc(S["root_ready"], 1)

            def fetch_table(i, func):
                act.activation(stat[:, 212 + i:213 + i], stats_of["x"][3][:, 0:1], func)

            for t in range(TT):
                act.wait_ge(S["ld_x"], 32)
                act.activation(spare[:, t * D:(t + 1) * D], h[:, t, :], ACT.Square,
                               accum_out=stats_of["x"][0][:, t:t + 1]).then_inc(S["x_sq"], 1)
            root("x", 2)
            act.wait_ge(S["ld_mem"], 16)
            for t in range(TT):
                act.activation(spare[:, t * D:(t + 1) * D], v_mem[:, t, :], ACT.Square,
                               accum_out=stats_of["mem"][0][:, t:t + 1]).then_inc(S["mem_sq"], 1)
            root("mem", 2)
            act.wait_ge(S["trig_in"], 1)
            act.activation(trig[:, 0:64], trig[:, 64:128], ACT.Sin).then_inc(S["sin_ready"], 1)
            act.wait_ge(S["x_done"], 1)
            for i in range(0, 8, 2):
                act.wait_ge(S["z_mm"], i + 1)
                act.activation(z[:, i // 4, (i % 4) * ZN:(i % 4 + 1) * ZN], bank[i][:, 0:ZN], ACT.Copy,
                               scale=stats_of["x"][3][:, i // 4:i // 4 + 1]).then_inc(S["z_act"], 1)
            act.wait_ge(S["z_act"], 4)
            act.wait_ge(S["z_vec"], 4)
            for t in range(TT):
                act.activation(spare[:, t * 512:t * 512 + QL], z[:, t, 3 * WA:3 * WA + QL], ACT.Square,
                               accum_out=stats_of["z"][0][:, t:t + 1]).then_inc(S["z_sq"], 1)
                act.activation(spare[:, t * 512 + QL:t * 512 + QL + KVL], z[:, t, 3 * WA + QL:3 * WA + QL + KVL],
                               ACT.Square, accum_out=stats_of["z"][0][:, 2 + t:3 + t]).then_inc(S["z_sq"], 1)
            root("z", 4)

            def mem_keys(j, b):
                act.wait_ge(S["kT_mm"], j + 1)
                act.activation(kT_mem[:, 2 * j:2 * j + 2, :], spl(bank[b][:, :], 2), ACT.Copy).then_inc(S["kT_ready"], 1)

            def mem_values_out(j, b):
                act.wait_ge(S["v_mm"], j + 1)
                t, n = divmod(j, 2)
                act.activation(v_mem[:, t, n * 512:(n + 1) * 512], bank[b][:, :], ACT.Copy).then_inc(S["v_ready"], 1)

            mem_keys(0, 6)
            mem_keys(1, 7)
            act.wait_ge(S["zroot_ready"], 1)
            for j in range(4):
                act.wait_ge(S["qb_mm"], j + 1)
                t, n = divmod(j, 2)
                act.activation(qb[:, t, n * 384:(n + 1) * 384], bank[j][:, 0:384], ACT.Copy,
                               scale=stats_of["z"][3][:, t:t + 1]).then_inc(S["qb_ready"], 1)
            for j in range(2):
                act.wait_ge(S["aT_mm"], j + 1)
                act.activation(qT_a[:, 2 * j:2 * j + 2, :], spl(bank[j][:, :], 2), ACT.Copy,
                               scale=DH ** -0.5).then_inc(S["qTa_ready"], 1)
            mem_keys(2, 4)
            mem_keys(3, 5)
            mem_values_out(0, 6)
            mem_values_out(1, 7)
            for j in range(4):
                act.wait_ge(S["q96_mm"], j + 1)
                act.activation(qT96[0:DQB, 2 * j:2 * j + 2, :], spl(bank[j][0:DQB, :], 2), ACT.Copy,
                               scale=DQB ** -0.5).then_inc(S["q96_ready"], 1)
            for j in range(4):
                act.wait_ge(S["k96_mm"], j + 1)
                act.activation(kT96[0:DQB, 2 * j:2 * j + 2, :], spl(bank[4 + j][0:DQB, :], 2), ACT.Copy).then_inc(S["k96_ready"], 1)
            mem_values_out(2, 4)
            mem_values_out(3, 5)

            def transposed(v):
                act.wait_ge(S["pT_mm"], v + 1)
                if v >= 2:
                    act.wait_ge(S["pv_mm"], v - 1)
                act.activation(probT[:, v % 2, :, :], spl(bank[2 + v % 2][:, :], 2), ACT.Copy).then_inc(S["pT_ready"], 1)

            def pair_out(c):
                act.wait_ge(S["pv_mm"], 2 * c + 2)
                act.activation(oT[:, c, :], bank[4 + c % 2][:, 0:SEQ], ACT.Copy, scale=gain[:, G_OUT + c:G_OUT + c + 1])\
                    .then_inc(S["oT_ready"], 1)
                if c >= 2:
                    act.wait_ge(S["oss_mm"], c - 1)
                act.activation(square_s[:, c % 2, :], bank[4 + c % 2][:, 0:SEQ], ACT.Square).then_inc(S["osq_ready"], 1)

            for u in range(NU + 6):
                if u < NU:
                    act.wait_ge(S["s_read"], u + 1)
                    if u >= NL:
                        act.wait_ge(S["pT_mm"], (u - NL) // TT + 1)
                    src = logit[:, u % NL, :] if u < NU // 2 else bank[(0, 1, 6)[u % 3]][:, 0:SEQ]
                    act.activation(prob[:, u % NL, :], src, ACT.Exp, bias=nmax[:, u:u + 1],
                                   accum_out=den[:, u:u + 1]).then_inc(S["e_ready"], 1)
                if u % 2 == 0 and 4 <= u and (u - 4) // 2 < 16:
                    transposed((u - 4) // 2)
                if u % 4 == 1 and u >= 9:
                    pair_out((u - 9) // 4)
            fetch_table(0, ACT.Sqrt)
            act.wait_ge(S["oss_mm"], 8)
            act.activation(oss_row[0:1, :], bank[7][0:1, :], ACT.Copy).then_inc(S["oss_ready"], 1)
            root("o", 4)
            for t in range(TT):
                act.wait_ge(S["h_ready"], 4 * t + 4)
                act.activation(square_early[:, t * D:(t + 1) * D], h[:, t, :], ACT.Square,
                               accum_out=stats_of["h"][0][:, t:t + 1]).then_inc(S["h_sq"], 1)
            root("h", 2)
            fetch_table(1, ACT.Exp)
            for j in range(4):
                act.wait_ge(S["qm_mm"], j + 1)
                act.activation(qT_m[:, 2 * j:2 * j + 2, :], spl(bank[4 + j][:, :], 2), ACT.Copy,
                               scale=MDH ** -0.5).then_inc(S["qm_ready"], 1)

            def mem_transposed(v):
                act.wait_ge(S["pmT_mm"], v + 1)
                if v >= 2:
                    act.wait_ge(S["om_mm"], v - 1)
                act.activation(probT_m[:, v % 2, :, :], spl(bank[2 + v % 2][:, :], 2), ACT.Copy).then_inc(S["pmT_ready"], 1)

            def mem_out(v):
                act.wait_ge(S["om_mm"], v + 1)
                act.activation(oT_m[:, 2 * v:2 * v + 2, :], spl(bank[4 + v % 2][:, :], 2), ACT.Copy).then_inc(S["om_ready"], 1)

            act.wait_ge(S["hroot_ready"], 1)
            for u in range(MH * TT):
                act.wait_ge(S["mmax_ready"], u + 1)
                if u >= NL:
                    act.wait_ge(S["pmT_mm"], (u - NL) // TT + 1)
                act.activation(prob_m[:, u % NL, :], bank[(0, 1, 6, 7)[u % 4]][:, 0:SEQ], ACT.Exp, bias=nm8[:, u:u + 1],
                               scale=stats_of["h"][3][:, u % TT:u % TT + 1],
                               accum_out=dn8[:, u:u + 1]).then_inc(S["em_ready"], 1)
                if u % TT == 1 and u >= 3:
                    mem_transposed(u // TT - 1)
                if u == 7:
                    mem_out(0)
            mem_transposed(MH - 1)
            for v in range(1, MH):
                mem_out(v)
            fetch_table(2, ACT.Sqrt)
            for t in range(TT):
                act.wait_ge(S["h2_ready"], 2 * t + 2)
                act.activation(square_late[:, t * D:(t + 1) * D], h[:, t, :], ACT.Square,
                               accum_out=stats_of["h2"][0][:, t:t + 1]).then_inc(S["h2_sq"], 1)
            root("h2", 2)
            fetch_table(3, ACT.Exp)
            for j in range(2):
                for t in range(TT):
                    if j:
                        act.wait_ge(S["split_vec" if t else "split_pool"], 1)
                    else:
                        act.wait_ge(S["xs_ready"], t + 1)
                    act.activation(part[j][:, t, :], rest[:, t, :], ACT.Copy).then_inc(S["split_act"], 1)
                if j == 0:
                    act.wait_ge(S["gate_in"], 1)
                    for t in range(TT):
                        act.activation(eg[:, t, :], top[:, t, 0:TOPK], ACT.Exp, bias=nmax0[:, t:t + 1],
                                       accum_out=esum[:, t:t + 1]).then_inc(S["gate_e"], 1)
            act.wait_ge(S["counts_ready"], 1)
            items = act.value_load(items_i[0:1, :], min_val=NE, max_val=NITEM - 1)
            with act.Fori(0, items) as w:
                act.wait_ge(S["gate_ready"], w + 1)
                act.activation(sig_s, gate_s, ACT.Sigmoid, scale=ALPHA).then_inc(S["sig_ready"], 1)
                act.wait_ge(S["hid_mm"], w + 1)
                act.activation(hT, bank[2][:, :], ACT.Copy).then_inc(S["hid_ready"], 1)
                act.wait_ge(S["chunks_used"], w * NCH + NCH)
                act.wait_ge(S["scattered"], w + 1)
                act.activation(o_s, bank[3][:, :], ACT.Copy).then_inc(S["out_copied"], 1)
                act.wait_ge(S["gsel_mm"], w + 1)
                act.activation(gsel, bank[2][:, 0:TT * P], ACT.Copy).then_inc(S["gsel_ready"], 1)
            fetch_table(4, ACT.Sqrt)
            for t in range(TT):
                act.wait_ge(S["f_ready"], 2 * t + 2)
                act.activation(spare[:, t * D:(t + 1) * D], h[:, t, :], ACT.Square,
                               accum_out=stats_of["f"][0][:, t:t + 1]).then_inc(S["f_sq"], 1)
            root("f", 2)

        @block.gpsimd
        def _(pool):
            for j in range(2):
                pool.wait_ge(S["split_act"], 2 * j + 1)
                left = part[2] if j else rest
                pool.tensor_tensor(left[:, 0, :], rest[:, 0, :], part[j][:, 0, :], ALU.subtract).then_inc(S["split_pool"], 1)

        @block.vector
        def _(dve):
            links = [0]

            def link(ins):
                links[0] += 1
                ins.then_inc(S["vec_chain"], 1)
                dve.wait_ge(S["vec_chain"], links[0])

            def mean_square(of, n, width):
                ss, ms = stats_of[of][0][:, 0:n], stats_of[of][1][:, 0:n]
                dve.tensor_scalar(ms, ss, 1.0 / width, EPS, ALU.mult, ALU.add).then_inc(S["ms_ready"], 1)

            def refine(of, n):
                ms, y0, rs = (a[:, 0:n] for a in stats_of[of][1:4])
                nw = nwt[:, 0:n]
                dve.wait_ge(S["root_ready"], NORMS.index(of) + 1)
                link(dve.reciprocal(y0, y0))
                link(dve.tensor_tensor(nw, ms, y0, ALU.mult))
                link(dve.tensor_tensor(nw, nw, y0, ALU.mult))
                link(dve.tensor_scalar(nw, nw, -0.5, 1.5, ALU.mult, ALU.add))
                link(dve.tensor_tensor(rs, nw, y0, ALU.mult))
                return rs

            def with_gain(dst, src, col, n, m):
                return dve.tensor_tensor(dst, src, over(gain[:, col:col + n].unsqueeze(2), [P, n, m]), ALU.mult)

            def gained(dst, mm, ready, col, banks, tiles=range(TT)):
                for i in [2 * t + b for t in tiles for b in range(2)]:
                    t, b = divmod(i, 2)
                    dve.wait_ge(mm, i + 1)
                    with_gain(dst[:, 4 * b:4 * b + 4, t * P:(t + 1) * P], spl(bank[banks[i]][:, :], 4),
                              col + 4 * b, 4, P).then_inc(ready, 1)

            dve.wait_ge(S["ld_cst"], 32)
            gained(nT, S["xT_mm"], S["xT_ready"], G_MIX, (0, 1, 2, 3))
            dve.wait_ge(S["x_sq"], 2)
            mean_square("x", 2, D)
            dve.wait_ge(S["ld_small"], 96)
            dve.tensor_copy(poscol[:, :], poscol_i[:, :])
            dve.tensor_copy(posrow[:, :], posrow_i[:, :])
            link(dve.tensor_copy(posk_f[:, :], posk_i[:, :]))

            def bucket_steps(half_no):
                n = SEQ // 8
                keys = posk_f[:, half_no * n:(half_no + 1) * n]
                dve.scalar_tensor_tensor(steps, over(keys.unsqueeze(2), [P, n, SEQ]), cst[:, C_STEP:C_STEP + 1],
                                         over(posrow[:, :].unsqueeze(1), [P, n, SEQ]), ALU.subtract,
                                         ALU.is_ge).then_inc(S["steps_ready"], 1)

            rs = refine("x", 2)
            dve.tensor_copy(mark[:, 3:4], rs[:, 0:1]).then_inc(S["x_done"], 1)
            ang, red, cnt_t = trig[:, 64:96], trig[:, 96:128], trig[:, 128:160]
            half = ROPE // 2
            for t in range(TT):
                link(dve.tensor_scalar(ang[:, t * half:(t + 1) * half], cst[:, C_FREQ:C_FREQ + half],
                                       poscol[:, t:t + 1], None, ALU.mult))
            magic = 12582912.0
            link(dve.tensor_scalar(cnt_t, ang, float(1 / (2 * np.pi)), magic, ALU.mult, ALU.add))
            link(dve.tensor_scalar(cnt_t, cnt_t, -magic, None, ALU.add))
            c1 = 6.28125
            c2 = float(np.float32(np.round((2 * np.pi - c1) * 2 ** 21) / 2 ** 21))
            c3 = float(2 * np.pi - c1 - c2)
            for c in (c1, c2, c3):
                link(dve.scalar_tensor_tensor(ang, cnt_t, -c, ang, ALU.mult, ALU.add))
            link(dve.tensor_scalar(ang, ang, 3.1415925, -3.1415925, ALU.min, ALU.max))
            link(dve.tensor_scalar(red, ang, -1.0, None, ALU.mult))
            link(dve.tensor_tensor(red, red, ang, ALU.max))
            dve.tensor_scalar(red, red, -1.0, float(np.pi / 2), ALU.mult, ALU.add).then_inc(S["trig_in"], 1)
            link(dve.tensor_tensor(relc[:, :], relc[:, :], relp[:, :], ALU.subtract))
            for j in range(3):
                link(dve.tensor_copy(delta[:, :, j], relc[:, :]))
                if j < 2:
                    link(dve.tensor_tensor(relc[:, :], relc[:, :], delta[:, :, j], ALU.subtract))
            link(dve.memset(ones_bf[:, :], 1.0))
            link(dve.memset(one[:, :], 1.0))
            dve.tensor_copy(up_bf[:, :], cst[:, C_UP:C_UP + P]).then_inc(S["ones_ready"], 1)
            bucket_steps(0)
            dve.wait_ge(S["mem_sq"], 2)
            mean_square("mem", 2, D)
            rs = refine("mem", 2)
            for t in range(TT):
                dve.tensor_scalar(v_mem[:, t, :], v_mem[:, t, :], rs[:, t:t + 1], None, ALU.mult).then_inc(S["memn_ready"], 1)
            for i in range(1, 8, 2):
                dve.wait_ge(S["z_mm"], i + 1)
                dve.tensor_scalar(z[:, i // 4, (i % 4) * ZN:(i % 4 + 1) * ZN], bank[i][:, 0:ZN],
                                  stats_of["x"][3][:, i // 4:i // 4 + 1], None, ALU.mult).then_inc(S["z_vec"], 1)
            gained(nT, S["mT_mm"], S["mT_ready"], G_MEM, (0, 1, 2, 3))
            dve.wait_ge(S["zT_mm"], 1)
            with_gain(znT[:, 0:2, :], spl(bank[4][:, :], 2), G_QA, 2, SEQ).then_inc(S["zT_ready"], 1)
            with_gain(znT[:, 2:3, :], spl(bank[5][:, 0:SEQ], 1), G_KVA, 1, SEQ).then_inc(S["zT_ready"], 1)
            dve.wait_ge(S["z_sq"], 4)
            ss, ms = stats_of["z"][0:2]
            dve.tensor_scalar(ms[:, 0:2], ss[:, 0:2], 1.0 / QL, EPS, ALU.mult, ALU.add)
            dve.tensor_scalar(ms[:, 2:4], ss[:, 2:4], 1.0 / KVL, EPS, ALU.mult, ALU.add).then_inc(S["ms_ready"], 1)
            rs = refine("z", 4)
            dve.tensor_copy(mark[:, 0:1], rs[:, 0:1]).then_inc(S["zroot_ready"], 1)
            for j in range(4):
                t, n = divmod(j, 2)
                dve.wait_ge(S["kvb_mm"], j + 1)
                src = bank[4 + j][:, :].rearrange("p (h n) -> p h n", h=4)
                kd = k96[:, t, :].rearrange("p (h n) -> p h n", h=HEADS)
                vd = v_b[:, t, :].rearrange("p (h n) -> p h n", h=HEADS)
                r = rs[:, 2 + t:3 + t]
                dve.tensor_scalar(kd[:, 4 * n:4 * n + 4, 0:NOPE], src[:, :, 0:NOPE], r, None, ALU.mult)
                dve.tensor_scalar(vd[:, 4 * n:4 * n + 4, :], src[:, :, NOPE:NOPE + DH], r, None, ALU.mult).then_inc(S["kvb_ready"], 1)
            for j in range(2):
                dve.wait_ge(S["aT_mm"], 3 + j)
                dve.tensor_copy(kT_a[:, 2 * j:2 * j + 2, :], spl(bank[2 + j][:, :], 2)).then_inc(S["kTa_ready"], 1)

            def rotary():
                dve.wait_ge(S["sin_ready"], 1)
                sin_c, cos_c = trig[:, 0:32], trig[:, 32:64]
                for t in range(TT):
                    dve.wait_ge(S["qb_ready"], 4)
                    qh = qb[:, t, :].rearrange("p (h n) -> p h n", h=HEADS)
                    kz = z[:, t, ZW - ROPE:ZW].unsqueeze(1)
                    kd = k96[:, t, :].rearrange("p (h n) -> p h n", h=HEADS)
                    for src, nh, base in ((qh, HEADS, NOPE), (kz, 1, 0)):
                        a, b = src[:, :, base:base + half], src[:, :, base + half:base + ROPE]
                        cb = over(cos_c[:, t * half:(t + 1) * half].unsqueeze(1), [P, nh, half])
                        sbc = over(sin_c[:, t * half:(t + 1) * half].unsqueeze(1), [P, nh, half])
                        tm = [rope_t[:, i * 128:i * 128 + nh * half].rearrange("p (h n) -> p h n", h=nh) for i in range(4)]
                        dve.tensor_tensor(tm[0], a, cb, ALU.mult)
                        dve.tensor_tensor(tm[1], b, sbc, ALU.mult)
                        dve.tensor_tensor(tm[2], a, sbc, ALU.mult)
                        link(dve.tensor_tensor(tm[3], b, cb, ALU.mult))
                        if nh > 1:
                            dve.tensor_tensor(a, tm[0], tm[1], ALU.subtract)
                            link(dve.tensor_tensor(b, tm[2], tm[3], ALU.add))
                        else:
                            full = [P, HEADS, half]
                            dve.tensor_tensor(kd[:, :, NOPE:NOPE + half], over(tm[0], full), over(tm[1], full), ALU.subtract)
                            dve.tensor_tensor(kd[:, :, NOPE + half:DQB], over(tm[2], full), over(tm[3], full),
                                              ALU.add).then_inc(S["ropek_ready"], 1)
                            dve.wait_ge(S["ropek_ready"], t + 1)

            def bias_out(f):
                hf, t, g, s = f // 16, f // 8 % 2, f // 2 % 4, f % 2
                dve.wait_ge(S["bias_mm"], f + 1)
                k0 = g * 64 + hf * 32 + s * 16
                dve.tensor_reduce(bias[:, t, :, k0:k0 + 16].rearrange("p h k -> p k h"),
                                  bank[f % 4][:, 0:384].rearrange("p (k h s) -> p k h s", k=16, s=3), X,
                                  ALU.add).then_inc(S["bias_ev"], 1)

            for f in range(16):
                bias_out(f)
            bucket_steps(1)
            rotary()
            for f in range(16, 32):
                bias_out(f)
            dve.wait_ge(S["bias_ev"], 32)
            for t in range(TT):
                link(dve.tensor_tensor(bias[:, t, :, :], bias[:, t, :, :],
                                       over(cst[:, C_LOGM + t * SEQ:C_LOGM + (t + 1) * SEQ].unsqueeze(1),
                                            [P, HEADS, SEQ]), ALU.add))

            for u in range(NU + 2):
                hd, t, late = u % 16 // TT, u % TT, u - 2
                src = bank[(0, 1, 6)[u % 3]][:, 0:SEQ]
                ins = None
                if u < NU:
                    dve.wait_ge(S["s_mm"], u + 1)
                if u < NU // 2:
                    if u >= NL:
                        dve.wait_ge(S["e_ready"], u - NL + 1)
                    ins = dve.tensor_tensor(logit[:, u % NL, :], src, bias[:, t, hd, :], ALU.add)
                elif u < NU:
                    dve.tensor_reduce(nmax[:, u:u + 1], src, X, ALU.max, negate=True).then_inc(S["s_read"], 1)
                if late >= 0:
                    dve.wait_ge(S["e_ready"], late + 1)
                    ins = dve.reciprocal(rden[:, late:late + 1], den[:, late:late + 1])
                if ins is not None:
                    link(ins)
                if u < NU // 2:
                    dve.tensor_reduce(nmax[:, u:u + 1], logit[:, u % NL, :], X, ALU.max, negate=True).then_inc(S["s_read"], 1)
                if late >= 0:
                    dve.tensor_scalar(prob[:, late % NL, :], prob[:, late % NL, :], rden[:, late:late + 1], None,
                                      ALU.mult).then_inc(S["p_ready"], 1)
            dve.wait_ge(S["ocol_mm"], 1)
            dve.tensor_scalar(stats_of["o"][1], bank[7][:, 0:4], 1.0 / WA, EPS, ALU.mult, ALU.add).then_inc(S["ms_ready"], 1)
            dve.wait_ge(S["ms_ready"], NORMS.index("o") + 1)
            dve.tensor_copy(mark[:, 1:2], stats_of["o"][1][:, 0:1]).then_inc(S["ocol_read"], 1)
            rs = refine("o", 4)
            for j in range(8):
                t, g, n = j // 4, j // 2 % 2, j % 2
                dve.wait_ge(S["wo_mm"], j + 1)
                if g:
                    dve.wait_ge(S["h_ready"], j - 1)
                hs = h[:, t, n * 512:(n + 1) * 512]
                dve.scalar_tensor_tensor(hs, bank[WO_BANKS[j]][:, :], rs[:, 2 * t + g:2 * t + g + 1], hs,
                                         ALU.mult, ALU.add).then_inc(S["h_ready"], 1)
            gained(hT_s, S["hT_mm"], S["hTs_ready"], G_X, (0, 1, 2, 3))
            dve.wait_ge(S["h_sq"], 2)
            mean_square("h", 2, D)
            rs = refine("h", 2)
            dve.tensor_copy(mark[:, 2:3], rs[:, 0:1]).then_inc(S["hroot_ready"], 1)

            def mem_normalise(u):
                dve.wait_ge(S["em_ready"], u + 1)
                link(dve.reciprocal(rd8[:, u:u + 1], dn8[:, u:u + 1]))
                dve.tensor_scalar(prob_m[:, u % NL, :], prob_m[:, u % NL, :], rd8[:, u:u + 1], None,
                                  ALU.mult).then_inc(S["pm_ready"], 1)

            for u in range(MH * TT + 1):
                if u < MH * TT:
                    dve.wait_ge(S["sm_mm"], u + 1)
                    link(dve.tensor_reduce(nm8[:, u:u + 1], bank[(0, 1, 6, 7)[u % 4]][:, 0:SEQ], X, ALU.max, negate=True))
                    dve.tensor_tensor(nm8[:, u:u + 1], nm8[:, u:u + 1], rs[:, u % TT:u % TT + 1], ALU.mult)\
                        .then_inc(S["mmax_ready"], 1)
                if u >= 1:
                    mem_normalise(u - 1)
            dve.wait_ge(S["ld_late"], 64)
            link(dve.tensor_copy(bgu[0:96, :], bgu_raw[0:96, :]))
            link(dve.tensor_tensor(bgu_raw[0:96, :], bgu_raw[0:96, :], bgu[0:96, :], ALU.subtract))
            dve.tensor_copy(bgu[32:64, :], bgu_raw[32:64, :])
            link(dve.tensor_copy(bgu[64:96, :], bgu_raw[64:96, :]))
            link(dve.tensor_tensor(bgu_raw[64:96, :], bgu_raw[64:96, :], bgu[64:96, :], ALU.subtract))
            link(dve.tensor_copy(bgu[64:96, :], bgu_raw[64:96, :]))
            for j in range(4):
                t, n = divmod(j, 2)
                dve.wait_ge(S["wm_mm"], j + 1)
                hs = h[:, t, n * 512:(n + 1) * 512]
                dve.tensor_tensor(hs, bank[(0, 1, 6, 7)[j]][:, :], hs, ALU.add).then_inc(S["h2_ready"], 1)
                if n:
                    gained(hT_s, S["h3T_mm"], S["h3T_ready"], G_MOE, (2, 3, 4, 5), (t,))
            dve.wait_ge(S["h2_sq"], 2)
            mean_square("h2", 2, D)
            rs = refine("h2", 2)
            for t in range(TT):
                dve.tensor_scalar(rest[:, t, :], h[:, t, :], rs[:, t:t + 1], None, ALU.mult).then_inc(S["xs_ready"], 1)
            for t in range(TT):
                dve.wait_ge(S["rt_mm"], t + 1)
                dve.scalar_tensor_tensor(lg[:, t, :], bank[6 + t][:, 0:NE], rs[:, t:t + 1], brow, ALU.mult, ALU.add)\
                    .then_inc(S["rt_read"], 1)
            dve.wait_ge(S["rt_read"], 2)
            both = range(TT)
            for t in both:
                ins = dve.max(top[:, t, :], lg[:, t, :])
            link(ins)
            for t in both:
                ins = dve.max_index(topi[:, t, :], top[:, t, :], lg[:, t, :])
            link(ins)
            dve.tensor_scalar(nmax0, top[:, :, 0], -1.0, None, ALU.mult).then_inc(S["gate_in"], 1)
            link(dve.tensor_copy(topf, topi))
            for t in both:
                ins = dve.tensor_tensor(oh[t], over(cst[:, C_EXP:C_EXP + NE].unsqueeze(1), [P, TOPK, NE]),
                                        over(topf[:, t, 0:TOPK].unsqueeze(2), [P, TOPK, NE]), ALU.is_equal)
            link(ins)
            for t in both:
                ins = dve.tensor_reduce(mask[:, t, :], oh[t].rearrange("p j e -> p e j"), X, ALU.add)
            link(ins)
            dve.tensor_copy(mask_bf, mask).then_inc(S["mask_ready"], 1)

            def split(j):
                dve.wait_ge(S["split_act"], 2 * j + 2)
                left = part[2] if j else rest
                dve.tensor_tensor(left[:, 1, :], rest[:, 1, :], part[j][:, 1, :], ALU.subtract).then_inc(S["split_vec"], 1)

            link(dve.tensor_scalar(place_e, mask, BIG, -BIG, ALU.mult, ALU.add))
            split(0)
            dve.wait_ge(S["rank_mm"], 1)
            link(dve.tensor_tensor(place_e, spl(bank[0][:, 0:2 * NE], 2), place_e, ALU.add))

            def choose(w, places=place):
                for t in range(TT):
                    ins = dve.tensor_scalar(pick[:, t, :], iota[:, 0:BLK], places[:, t, bass.ds(w, 1)], None, ALU.is_equal)
                ins.then_inc(S["pick_ready"], 1)

            def choose_bias(w, experts=onehot):
                dve.tensor_copy(bsel[0:96, :], over(experts[0:96, bass.ds(w, 1)], [96, BLK])).then_inc(S["bsel_ready"], 1)

            def gathered_out(w):
                dve.wait_ge(S["gathered"], w + 1)
                dve.tensor_tensor(spl(xgT, KC), spl(bank[2][:, :], KC),
                                  over(gain[:, G_MOE:G_MOE + KC].unsqueeze(2), [P, KC, BLK]), ALU.mult).then_inc(S["xg_ready"], 1)

            choose(0, place_e)
            choose_bias(0, cst[:, C_MOD:C_MOD + NE])
            split(1)
            link(dve.tensor_scalar(eid_f[:, 0:1], cst[:, C_ITEM:C_ITEM + 1], 0.0, None, ALU.add))
            dve.tensor_copy(eid_i[:, 0:1], eid_f[:, 0:1]).then_inc(S["first_ready"], 1)
            link(dve.tensor_copy(cnt, bank[0][:, 64:96]))
            link(dve.tensor_scalar(extra, cnt, float(BLK), None, ALU.is_gt))
            for m in range(2, SEQ // BLK):
                link(dve.scalar_tensor_tensor(extra, cnt, float(m * BLK), extra, ALU.is_gt, ALU.add))
            link(dve.tensor_reduce(total_f, extra, X, ALU.add))
            dve.tensor_scalar(items_i, total_f, float(NE), None, ALU.add).then_inc(S["counts_ready"], 1)
            dve.wait_ge(S["gate_e"], 2)
            link(dve.reciprocal(ersum, esum))
            for t in range(TT):
                link(dve.tensor_scalar(eg[:, t, :], eg[:, t, :], ersum[:, t:t + 1], None, ALU.mult))
                link(dve.tensor_tensor(oh[t], oh[t], over(eg[:, t, :].unsqueeze(2), [P, TOPK, NE]), ALU.mult))
                dve.tensor_reduce(gates_e[:, t, :], oh[t].rearrange("p j e -> p e j"), X, ALU.add).then_inc(S["gates_ready"], 1)
            dve.memset(o_s, 0.0).then_inc(S["out_copied"], 1)
            dve.memset(gsel, 0.0).then_inc(S["gsel_ready"], 1)
            link(dve.tensor_scalar(cum, extra, 1.0, None, ALU.add))
            a, b = cum, cum2
            for s in (1, 2, 4, 8, 16):
                dve.tensor_copy(b[:, 0:s], a[:, 0:s])
                link(dve.tensor_tensor(b[:, s:NE], a[:, s:NE], a[:, 0:NE - s], ALU.add))
                a, b = b, a
            ends = a
            dve.tensor_scalar(last_i, ends, -1.0, None, ALU.add).then_inc(S["ends_ready"], 1)
            dve.wait_ge(S["gtT_mm"], 1)
            dve.tensor_copy(gT[0:NE, :], bank[3][0:NE, 0:SEQ]).then_inc(S["gtT_ready"], 1)
            gathered_out(0)
            link(dve.tensor_tensor(beg, ends, extra, ALU.subtract))
            link(dve.tensor_scalar(beg, beg, float(BLK), -float(BLK), ALU.mult, ALU.add))
            item = cst[:, C_ITEM:C_ITEM + NITEM]
            full = [P, NITEM, NE]
            link(dve.tensor_tensor(val, over(item.unsqueeze(2), full), over(ends.unsqueeze(1), full), ALU.is_ge))
            link(dve.tensor_reduce(eid_f, val, X, ALU.add))
            dve.tensor_copy(eid_i[:, 1:NITEM], eid_f[:, 1:NITEM])
            dve.tensor_scalar(onehot, eid_f, cst[:, C_PMOD:C_PMOD + 1], None, ALU.is_equal)
            link(dve.tensor_tensor(own, over(eid_f.unsqueeze(2), full),
                                   over(cst[:, C_EXP:C_EXP + NE].unsqueeze(1), full), ALU.is_equal))

            def pick_out(dst, row):
                link(dve.tensor_tensor(val, own, over(row.unsqueeze(1), full), ALU.mult))
                return dve.tensor_reduce(dst, val, X, ALU.add)

            for t in range(TT):
                link(dve.tensor_tensor(cnt, place_e[:, t, :], beg, ALU.add))
                link(pick_out(place[:, t, :], cnt))
                link(dve.scalar_tensor_tensor(place[:, t, :], item, -float(BLK), place[:, t, :], ALU.mult, ALU.add))
                ins = pick_out(gates[:, t, :], gates_e[:, t, :])
                link(ins) if t == 0 else ins.then_inc(S["tables_ready"], 1)
            dve.wait_ge(S["tables_ready"], 1)
            dve.wait_ge(S["counts_ready"], 1)
            items = dve.value_load(items_i[0:1, :], min_val=NE, max_val=NITEM - 1)
            with dve.Fori(0, items) as w:
                nxt = w + 1
                dve.wait_ge(S["gathered"], w + 1)
                choose(nxt)
                dve.wait_ge(S["chunks_used"], w * NCH + 1)
                choose_bias(nxt)
                for t in range(TT):
                    ins = dve.tensor_scalar(gtok[:, t, :], iota, place[:, t, bass.ds(w, 1)],
                                            gates[:, t, bass.ds(w, 1)], ALU.is_equal, ALU.mult)
                ins.then_inc(S["gtok_ready"], 1)
                dve.wait_ge(S["chunks_used"], w * NCH + NGU)
                dve.tensor_scalar(gate_s, bank[0][:, :], LIMIT, None, ALU.min).then_inc(S["gate_ready"], 1)
                dve.tensor_scalar(up_s, bank[1][:, :], LIMIT, -LIMIT, ALU.min, ALU.max).then_inc(S["up_ready"], 1)
                dve.wait_ge(S["gate_ready"], w + 1)
                dve.wait_ge(S["up_ready"], w + 1)
                dve.scalar_tensor_tensor(up_s, up_s, 1.0, gate_s, ALU.add, ALU.mult).then_inc(S["gu_ready"], 1)
                dve.wait_ge(S["sig_ready"], w + 1)
                dve.wait_ge(S["gu_ready"], w + 1)
                dve.tensor_tensor(h_s, up_s, sig_s, ALU.mult).then_inc(S["hmid_ready"], 1)
                gathered_out(nxt)
            dve.wait_ge(S["y_done"], 1)
            for j in range(4):
                t, n = divmod(j, 2)
                dve.tensor_tensor(h[:, t, n * 512:(n + 1) * 512], bank[4 + j][:, :], h[:, t, n * 512:(n + 1) * 512],
                                  ALU.add).then_inc(S["f_ready"], 1)
            dve.wait_ge(S["f_sq"], 2)
            mean_square("f", 2, D)
            rs = refine("f", 2)
            dve.wait_ge(S["ld_row"], 16)
            for t in range(TT):
                dve.scalar_tensor_tensor(h[:, t, :], h[:, t, :], rs[:, t:t + 1], g_row.rearrange("p c n -> p (c n)"), ALU.mult,
                                         ALU.mult).then_inc(S["fin_ready"], 1)

        @block.tensor
        def _(pe):
            mm = pe.matmul

            def transposes(src, ready, per, done, banks, tiles=range(TT)):
                for t in tiles:
                    if ready:
                        pe.wait_ge(ready, per * (t + 1))
                    for b in range(2):
                        for j in range(4):
                            c = 4 * b + j
                            ins = pe.transpose(bank[banks[2 * t + b]][:, j * P:(j + 1) * P],
                                               src[:, t, c * P:(c + 1) * P], ident)
                        ins.then_inc(done, 1)

            pe.wait_ge(S["ld_id"], 16)
            pe.wait_ge(S["ld_x"], 32)
            transposes(h, None, 0, S["xT_mm"], (0, 1, 2, 3))
            pe.wait_ge(S["xT_ready"], 4)
            for k in range(KC):
                pe.wait_ge(ld_win[k], 16)
                for t in range(TT):
                    for n in range(4):
                        ins = mm(bank[4 * t + n][:, 0:ZN], nT[:, k, t * P:(t + 1) * P], win[:, k, n * ZN:(n + 1) * ZN],
                                 start=(k == 0), stop=(k == KC - 1))
                        if k == KC - 1:
                            ins.then_inc(S["z_mm"], 1)
            pe.wait_ge(S["z_act"], 2)
            pe.wait_ge(S["z_vec"], 2)
            transposes(v_mem, S["memn_ready"], 1, S["mT_mm"], (0, 1, 2, 3))
            pe.wait_ge(S["z_act"], 4)
            pe.wait_ge(S["z_vec"], 4)
            for c in range(3):
                for t in range(TT):
                    ins = pe.transpose(bank[4 + c // 2][:, c % 2 * SEQ + t * P:c % 2 * SEQ + (t + 1) * P],
                                       z[:, t, 3 * WA + c * P:3 * WA + (c + 1) * P], ident)
            ins.then_inc(S["zT_mm"], 1)

            def mem_keys(c, b):
                for k in range(KC):
                    if c == 0:
                        pe.wait_ge(ld_ring[k], 16)
                    ins = mm(bank[b][:, c % 2 * SEQ:(c % 2 + 1) * SEQ], wmkv[:, k, c * P:(c + 1) * P], nT[:, k, :],
                             start=(k == 0), stop=(k == KC - 1))
                if c % 2:
                    ins.then_inc(S["kT_mm"], 1)

            def mem_values_in(t, banks):
                for n in range(2):
                    for k in range(KC):
                        ins = mm(bank[banks[n]][:, :], nT[:, k, t * P:(t + 1) * P], wmkv[:, k, D + n * 512:D + (n + 1) * 512],
                                 start=(k == 0), stop=(k == KC - 1))
                    ins.then_inc(S["v_mm"], 1)

            pe.wait_ge(S["mT_ready"], 4)
            for c in range(4):
                mem_keys(c, 6 + c // 2)
            pe.wait_ge(S["zT_ready"], 2)
            pe.wait_ge(S["ld_lora"], 32)
            for t in range(TT):
                for n in range(2):
                    for k in range(2):
                        ins = mm(bank[2 * t + n][:, 0:384], znT[:, k, t * P:(t + 1) * P], wqb[:, k, n * 384:(n + 1) * 384],
                                 start=(k == 0), stop=(k == 1))
                    ins.then_inc(S["qb_mm"], 1)
            pe.wait_ge(S["kT_ready"], 2)
            for t in range(TT):
                for n in range(2):
                    mm(bank[4 + 2 * t + n][:, :], znT[:, 2, t * P:(t + 1) * P], wkvb[:, n * 512:(n + 1) * 512],
                       start=True, stop=True).then_inc(S["kvb_mm"], 1)
            for c in range(8):
                if c % 2 == 0:
                    pe.wait_ge(S["qb_ready"], c // 2 + 1)
                for t in range(TT):
                    ins = pe.transpose(bank[c // 2][:, c % 2 * SEQ + t * P:c % 2 * SEQ + (t + 1) * P],
                                       z[:, t, c * P:(c + 1) * P], ident)
                if c % 2:
                    ins.then_inc(S["aT_mm"], 1)
            pe.wait_ge(S["kvb_ready"], 2)
            for c in range(4, 8):
                mem_keys(c, 2 + c // 2)

            def bias_fill(f):
                hf, t, g, s = f // 16, f // 8 % 2, f // 2 % 4, f % 2
                if f >= 4:
                    pe.wait_ge(S["bias_ev"], f - 3)
                for k in range(16):
                    ins = mm(bank[f % 4][:, 24 * k:24 * k + 24], steps[32 * g:32 * g + 32, s * 16 + k, t * P:(t + 1) * P],
                             delta[32 * g:32 * g + 32, :, :], start=True, stop=True)
                ins.then_inc(S["bias_mm"], 1)

            pe.wait_ge(S["qTa_ready"], 2)
            pe.wait_ge(S["kTa_ready"], 2)
            pe.wait_ge(S["steps_ready"], 1)
            for f in range(16):
                bias_fill(f)
            pe.wait_ge(S["kvb_ready"], 4)
            mem_values_in(0, (6, 7))
            pe.wait_ge(S["steps_ready"], 2)
            for f in range(16, 32):
                bias_fill(f)
            pe.wait_ge(S["ropek_ready"], 2)
            pe.wait_ge(S["bias_ev"], 32)
            for src, first, done in ((qb, 0, S["q96_mm"]), (k96, 4, S["k96_mm"])):
                if first:
                    pe.wait_ge(S["kT_ready"], 4)
                    pe.wait_ge(S["v_ready"], 2)
                for j in range(4):
                    for hd in (2 * j, 2 * j + 1):
                        for t in range(TT):
                            ins = pe.transpose(bank[first + j][0:DQB, hd % 2 * SEQ + t * P:hd % 2 * SEQ + (t + 1) * P],
                                               src[:, t, hd * DQB:(hd + 1) * DQB], ident)
                    ins.then_inc(done, 1)
            pe.wait_ge(S["k96_ready"], 2)
            mem_values_in(1, (4, 5))

            def scores(u):
                a, hd, t = u // 16, u % 16 // TT, u % TT
                if u >= 3:
                    pe.wait_ge(S["s_read"], u - 2)
                    if u - 3 >= NU // 2:
                        pe.wait_ge(S["e_ready"], u - 2)
                if a == 0:
                    lo = hd % 2 * DH
                    q, k = qT_a[lo:lo + DH, hd // 2, t * P:(t + 1) * P], kT_a[lo:lo + DH, hd // 2, :]
                else:
                    q, k = qT96[0:DQB, hd, t * P:(t + 1) * P], kT96[0:DQB, hd, :]
                mm(bank[(0, 1, 6)[u % 3]][:, 0:SEQ], q, k, start=True, stop=True).then_inc(S["s_mm"], 1)

            def probs_transposed(u):
                v, t = divmod(u, TT)
                pe.wait_ge(S["p_ready"], u + 1)
                if t == 0 and v >= 2:
                    pe.wait_ge(S["pT_ready"], v - 1)
                for m in range(TT):
                    ins = pe.transpose(bank[2 + v % 2][:, m * SEQ + t * P:m * SEQ + (t + 1) * P],
                                       prob[:, u % NL, m * P:(m + 1) * P], ident)
                if t:
                    ins.then_inc(S["pT_mm"], 1)

            def outputs(v):
                a, hd = divmod(v, HEADS)
                lo, c = v % 2 * DH, v // 2
                pe.wait_ge(S["pT_ready"], v + 1)
                if v % 2 == 0 and c >= 2:
                    pe.wait_ge(S["osq_ready"], c - 1)
                for m in range(TT):
                    vv = z[:, m, 2 * WA + hd * DH:2 * WA + (hd + 1) * DH] if a == 0 else v_b[:, m, hd * DH:(hd + 1) * DH]
                    ins = mm(bank[4 + c % 2][lo:lo + DH, 0:SEQ], vv, probT[:, v % 2, m, :], start=(m == 0), stop=(m == TT - 1))
                ins.then_inc(S["pv_mm"], 1)

            def square_sums(c):
                pe.wait_ge(S["osq_ready"], c + 1)
                a = c // 4
                mm(bank[7][0:1, a * SEQ:(a + 1) * SEQ], one[:, :], square_s[:, c % 2, :],
                   start=(c % 4 == 0), stop=(c % 4 == 3)).then_inc(S["oss_mm"], 1)

            pe.wait_ge(S["q96_ready"], 4)
            pe.wait_ge(S["k96_ready"], 4)
            pe.wait_ge(S["v_ready"], 2)
            for i in range(NU + 10):
                if i < NU:
                    scores(i)
                if 0 <= i - 3 < NU:
                    probs_transposed(i - 3)
                if i % 2 == 0 and 0 <= (i - 6) // 2 < 16:
                    if i == 6:
                        pe.wait_ge(S["v_ready"], 4)
                    outputs((i - 6) // 2)
                if i % 4 == 3 and 0 <= (i - 11) // 4 < 8:
                    square_sums((i - 11) // 4)

            pe.wait_ge(S["ld_wo"], 16)
            pe.wait_ge(S["oT_ready"], 8)
            for j in range(8):
                t, g, n = j // 4, j // 2 % 2, j % 2
                if j == 1:
                    pe.wait_ge(S["oss_ready"], 1)
                    for tt in range(TT):
                        for a in range(2):
                            ins = mm(bank[7][:, 2 * tt + a:2 * tt + a + 1], oss_row[0:1, a * SEQ + tt * P:a * SEQ + (tt + 1) * P],
                                     one[0:1, :], start=True, stop=True)
                    ins.then_inc(S["ocol_mm"], 1)
                if j == 7:
                    pe.wait_ge(S["ocol_read"], 1)
                for k in range(4):
                    ins = mm(bank[WO_BANKS[j]][:, :], oT[:, 4 * g + k, t * P:(t + 1) * P],
                             wo[:, 4 * g + k, n * 512:(n + 1) * 512], start=(k == 0), stop=(k == 3))
                ins.then_inc(S["wo_mm"], 1)
            transposes(h, S["h_ready"], 4, S["hT_mm"], (0, 1, 2, 3))
            pe.wait_ge(S["hTs_ready"], 4)
            pe.wait_ge(S["ld_wmq"], 16)
            for c in range(KC):
                for k in range(KC):
                    ins = mm(bank[4 + c // 2][:, c % 2 * SEQ:(c % 2 + 1) * SEQ], wmq[:, k, c * P:(c + 1) * P], hT_s[:, k, :],
                             start=(k == 0), stop=(k == KC - 1))
                if c % 2:
                    ins.then_inc(S["qm_mm"], 1)

            def mem_scores(u):
                hd, t = divmod(u, TT)
                if u < MH:
                    pe.wait_ge(S["qm_ready"], u + 1 if u >= 2 else hd + 1)
                if u in (2, 3):
                    pe.wait_ge(S["qm_ready"], 4)
                if u >= 4:
                    pe.wait_ge(S["em_ready"], u - 3)
                for j in range(2):
                    c = 2 * hd + j
                    ins = mm(bank[(0, 1, 6, 7)[u % 4]][:, 0:SEQ], qT_m[:, c, t * P:(t + 1) * P], kT_mem[:, c, :],
                             start=(j == 0), stop=(j == 1))
                ins.then_inc(S["sm_mm"], 1)

            def mem_probs(hd):
                pe.wait_ge(S["pm_ready"], 2 * hd + 2)
                if hd >= 2:
                    pe.wait_ge(S["pmT_ready"], hd - 1)
                for t in range(TT):
                    for m in range(TT):
                        ins = pe.transpose(bank[2 + hd % 2][:, m * SEQ + t * P:m * SEQ + (t + 1) * P],
                                           prob_m[:, (2 * hd + t) % NL, m * P:(m + 1) * P], ident)
                ins.then_inc(S["pmT_mm"], 1)

            def mem_values(hd):
                pe.wait_ge(S["pmT_ready"], hd + 1)
                if hd >= 2:
                    pe.wait_ge(S["om_ready"], hd - 1)
                for j in range(2):
                    for m in range(TT):
                        c = 2 * hd + j
                        ins = mm(bank[4 + hd % 2][:, j * SEQ:(j + 1) * SEQ], v_mem[:, m, c * P:(c + 1) * P],
                                 probT_m[:, hd % 2, m, :], start=(m == 0), stop=(m == TT - 1))
                ins.then_inc(S["om_mm"], 1)

            mem_scores(0)
            mem_scores(1)
            for hd in range(MH):
                if hd + 1 < MH:
                    mem_scores(2 * hd + 2)
                    mem_scores(2 * hd + 3)
                mem_probs(hd)
                if hd >= 1:
                    mem_values(hd - 1)
            mem_values(MH - 1)
            pe.wait_ge(S["om_ready"], MH)
            pe.wait_ge(S["ld_wmo"], 16)
            for j in range(4):
                t, n = divmod(j, 2)
                for k in range(KC):
                    ins = mm(bank[(0, 1, 6, 7)[j]][:, :], oT_m[:, k, t * P:(t + 1) * P],
                             wmo[:, k, n * 512:(n + 1) * 512], start=(k == 0), stop=(k == KC - 1))
                ins.then_inc(S["wm_mm"], 1)
                if j == 2:
                    transposes(h, S["h2_ready"], 2, S["h3T_mm"], (2, 3, 4, 5), (0,))
            pe.wait_ge(S["ld_wr"], 16)
            transposes(h, S["h2_ready"], 2, S["h3T_mm"], (2, 3, 4, 5), (1,))
            for t in range(TT):
                pe.wait_ge(S["h3T_ready"], 2 * t + 2)
                for k in range(KC):
                    ins = mm(bank[6 + t][:, 0:NE], hT_s[:, k, t * P:(t + 1) * P], wr[:, k, :], start=(k == 0), stop=(k == KC - 1))
                ins.then_inc(S["rt_mm"], 1)
            pe.wait_ge(S["mask_ready"], 1)
            pe.wait_ge(S["ones_ready"], 1)
            mm(bank[0][:, 0:32], up_bf[:, :], mask_bf[:, 0, :], start=True, stop=True)
            mm(bank[0][:, 32:64], ones_bf[:, :], mask_bf[:, 0, :], start=True, stop=False)
            mm(bank[0][:, 32:64], up_bf[:, :], mask_bf[:, 1, :], start=False, stop=True)
            mm(bank[0][:, 64:96], ones_bf[:, :], mask_bf[:, 0, :], start=True, stop=False)
            mm(bank[0][:, 64:96], ones_bf[:, :], mask_bf[:, 1, :], start=False, stop=True).then_inc(S["rank_mm"], 1)

            def gather():
                for c in range(KC):
                    for j in range(3):
                        for t in range(TT):
                            ins = mm(bank[2][:, c * BLK:(c + 1) * BLK], part[j][:, t, c * P:(c + 1) * P], pick[:, t, :],
                                     start=(j == 0 and t == 0), stop=(j == 2 and t == TT - 1))
                ins.then_inc(S["gathered"], 1)

            def scatter(last=False):
                for t in range(TT):
                    for n in range(2):
                        lo = n * BLK
                        ins = mm(bank[4 + 2 * t + n][:, :], gsel[lo:lo + BLK, t * P:(t + 1) * P], o_s[lo:lo + BLK, :],
                                 start=False, stop=last, skip_group_check=True)
                return ins

            pe.wait_ge(S["split_act"], 4)
            pe.wait_ge(S["split_pool"], 2)
            pe.wait_ge(S["split_vec"], 2)
            pe.wait_ge(S["pick_ready"], 1)
            gather()
            pe.wait_ge(S["gates_ready"], 2)
            for t in range(TT):
                ins = pe.transpose(bank[3][0:NE, t * P:(t + 1) * P], gates_e[:, t, :], ident)
            ins.then_inc(S["gtT_mm"], 1)
            pe.wait_ge(S["gtT_ready"], 1)
            pe.wait_ge(S["ld_late"], 64)
            for t in range(TT):
                for n in range(2):
                    mm(bank[4 + 2 * t + n][:, :], gT[0:NE, t * P:(t + 1) * P], bdn[0:NE, n * 512:(n + 1) * 512],
                       start=True, stop=False, skip_group_check=True)
            pe.wait_ge(S["counts_ready"], 1)
            pe.wait_ge(S["first_ready"], 1)
            items = pe.value_load(items_i[0:1, :], min_val=NE, max_val=NITEM - 1)
            with pe.Fori(0, items) as w:
                nxt = w + 1
                e = pe.value_load(eid_i[0:1, bass.ds(w, 1)], min_val=0, max_val=NE - 1)
                pe.wait_ge(S["xg_ready"], nxt)
                pe.wait_ge(S["bsel_ready"], nxt)
                for n in range(4):
                    lo = n % 2 * BLK
                    mm(bank[n // 2][lo:lo + BLK, :], bsel[0:96, :], bgu[0:96, n * 512:(n + 1) * 512], start=True, stop=False)
                for k in range(NGU):
                    pe.wait_ge(ld_ring[k], e * 16 + 32)
                    for n in range(4):
                        lo = n % 2 * BLK
                        ins = mm(bank[n // 2][lo:lo + BLK, :], xgT[:, k * BLK:(k + 1) * BLK],
                                 slot(k)[:, n * 512:(n + 1) * 512], start=False, stop=(k == NGU - 1))
                    ins.then_inc(S["chunks_used"], 1)
                pe.wait_ge(S["gsel_ready"], nxt)
                pe.wait_ge(S["pick_ready"], w + 2)
                gather()
                pe.wait_ge(S["out_copied"], nxt)
                scatter().then_inc(S["scattered"], 1)
                pe.wait_ge(S["xg_ready"], w + 2)
                pe.wait_ge(S["hmid_ready"], nxt)
                for j in range(4):
                    ins = pe.transpose(bank[2][:, j * P:(j + 1) * P], h_s[:, j * P:(j + 1) * P], ident)
                ins.then_inc(S["hid_mm"], 1)
                pe.wait_ge(S["hid_ready"], nxt)
                for c in range(NDN):
                    pe.wait_ge(ld_ring[NGU + c], e * 16 + 16)
                    for j in range(2):
                        f = 2 * c + j
                        lhs = hT[:, f % 4 * P + f // 4 * BLK:f % 4 * P + f // 4 * BLK + BLK]
                        for n in range(2):
                            ins = mm(bank[3][n * BLK:(n + 1) * BLK, :], lhs,
                                     slot(NGU + c)[:, j * D + n * 512:j * D + (n + 1) * 512],
                                     start=(f == 0), stop=(f == 7))
                    ins.then_inc(S["chunks_used"], 1)
                pe.wait_ge(S["gtok_ready"], nxt)
                for t in range(TT):
                    ins = pe.transpose(bank[2][:, t * P:(t + 1) * P], gtok[:, t, :], ident)
                ins.then_inc(S["gsel_mm"], 1)
            pe.wait_ge(S["out_copied"], items + 1)
            pe.wait_ge(S["gsel_ready"], items + 1)
            scatter(last=True).then_inc(S["y_done"], 1)


def kernel(x, mem, positions, g_mix, w_in, g_q_a, w_q_b, g_kv_a, w_kv_b, rel_bias, g_out_a, g_out_b, w_o,
           g_xattn, g_mem, w_mq, w_mkv, w_mo, g_moe, w_router, b_router, w_gate_up, b_gate_up, w_down,
           b_down, g_final):
    import concourse.bacc as bacc
    from concourse.bass_utils import run_bass_kernel_spmd

    def cols(g):
        return np.asarray(g).reshape(-1, P).T

    pos = np.ascontiguousarray(np.asarray(positions)[0])
    rel = np.asarray(rel_bias)
    rel_cur = np.concatenate([rel[ORDER], rel[:1]])
    rel_prev = np.concatenate([np.zeros((1, HEADS), rel.dtype), rel[ORDER]])
    ins = {
        "x": np.asarray(x)[0], "mem": np.asarray(mem)[0], "pos": pos, "pos_col": pos.reshape(TT, P).T,
        "posk": np.repeat(pos.reshape(4, SEQ // 4), NB, axis=0),
        "consts": shape_constants(),
        "gains": np.concatenate([cols(g_mix), cols(g_xattn), cols(g_mem), cols(g_moe), cols(g_out_a),
                                 cols(g_out_b), cols(g_q_a), cols(g_kv_a)], axis=1),
        "w_in": w_in[0], "w_q_b": w_q_b[0], "w_kv_b": w_kv_b[0],
        "rel_cur": np.tile(rel_cur, (P // NB, 1)), "rel_prev": np.tile(rel_prev, (P // NB, 1)),
        "w_o": w_o[0], "w_mq": w_mq[0], "w_mkv": w_mkv[0], "w_mo": w_mo[0],
        "w_router": w_router[0], "b_router": b_router[0], "w_gate_up": w_gate_up[0],
        "b_gate_up": b_gate_up[0], "w_down": w_down[0], "b_down": b_down[0], "g_final": g_final,
    }
    nc = bacc.Bacc("TRN2", target_bir_lowering=False, num_devices=1)
    arrays, args = {}, []
    for name, a in ins.items():
        a = np.ascontiguousarray(a)
        arrays[f"in_{name}"] = a
        args.append(nc.dram_tensor(f"in_{name}", a.shape, mybir.dt.from_np(a.dtype), kind="ExternalInput").ap())
    args.append(nc.dram_tensor("out", (SEQ, D), mybir.dt.float32, kind="ExternalOutput").ap())
    encoder_kernel(nc, *args)
    r = run_bass_kernel_spmd(nc, [arrays], core_ids=[0])
    return r.results[0]["out"].reshape(1, SEQ, D)
```
